# Optimizing a Trainium2 kernel written in Bass

```python
import jax, jax.numpy as jnp
from jax import lax
import numpy as np

D_MODEL = 1024
BATCH = 1
SEQ = 1024
DEPTH = 2

N_MIXERS = 2
EPS = 1e-6

A_HEADS = 16
A_KV_HEADS = 4
A_HEAD_DIM = D_MODEL // A_HEADS
A_WIDTH = A_HEADS * A_HEAD_DIM
A_KV_WIDTH = A_KV_HEADS * A_HEAD_DIM
WINDOW = 128
BLOCK = WINDOW
A_IN = 2 * A_WIDTH + 2 * A_KV_WIDTH

B_HEADS = 8
B_HEAD_K = 128
B_HEAD_V = 128
B_KW = B_HEADS * B_HEAD_K
B_VW = B_HEADS * B_HEAD_V
CONV_WIDTH = 5
CHUNK = 64
B_IN = 2 * B_KW + 2 * B_VW + 4 * B_HEADS

kernel_name = "hybrid_swa_sink_alibi_gated_deltanet_bidir"

def rms_norm(x, g):
    xf = x.astype(jnp.float32)
    y = xf * lax.rsqrt(jnp.mean(xf * xf, axis=-1, keepdims=True) + EPS)
    return (y * g.astype(jnp.float32)).astype(x.dtype)

def l2_norm(x):
    return x * lax.rsqrt(jnp.sum(x * x, axis=-1, keepdims=True) + EPS)

def alibi_slopes(n_heads):
    return jnp.asarray(np.power(2.0, -8.0 * np.arange(1, n_heads + 1) / n_heads), dtype=jnp.float32)

def windowed_gqa_sink(q, k, v, sink):
    b, s, _ = q.shape
    g, r, dh = A_KV_HEADS, A_HEADS // A_KV_HEADS, A_HEAD_DIM
    nb = s // BLOCK
    f32 = jnp.float32
    qb = q.astype(f32).reshape(b, nb, BLOCK, g, r, dh)

    def band(t):
        tp = jnp.pad(t.astype(f32).reshape(b, s, g, dh), ((0, 0), (BLOCK, BLOCK), (0, 0), (0, 0)))
        tp = tp.reshape(b, nb + 2, BLOCK, g, dh)
        return jnp.concatenate([tp[:, :-2], tp[:, 1:-1], tp[:, 2:]], axis=2)

    kb, vb = band(k), band(v)
    qpos = jnp.arange(BLOCK)[:, None]
    krel = jnp.arange(3 * BLOCK)[None, :] - BLOCK
    dist = jnp.abs(krel - qpos)
    kabs = jnp.arange(nb)[:, None] * BLOCK + krel
    valid = (dist <= WINDOW)[None] & ((kabs >= 0) & (kabs < s))[:, None, :]
    slopes = alibi_slopes(A_HEADS).reshape(g, r)
    alibi = -slopes[:, :, None, None] * dist.astype(f32)
    bias = jnp.where(valid[:, None, None], alibi[None], -jnp.inf)

    scores = jnp.einsum('bnqgrd,bnkgd->bngrqk', qb, kb) * (dh ** -0.5) + bias[None]
    sk = sink.astype(f32).reshape(g, r)[None, None, :, :, None]
    m = jnp.maximum(jnp.max(scores, axis=-1), sk)
    p = jnp.exp(scores - m[..., None])
    denom = jnp.sum(p, axis=-1) + jnp.exp(sk - m)
    o = jnp.einsum('bngrqk,bnkgd->bnqgrd', p, vb)
    o = o / jnp.transpose(denom, (0, 1, 4, 2, 3))[..., None]
    return o.reshape(b, s, g * r * dh)

def short_conv_centred(x, w):
    pad = w.shape[0] // 2
    return lax.conv_general_dilated(
        x, w[:, None, :].astype(x.dtype), window_strides=(1,), padding=[(pad, pad)],
        dimension_numbers=('NWC', 'WIO', 'NWC'), feature_group_count=x.shape[-1])

def gated_delta_chunked(q, k, v, g, beta):
    b, s, h, dk = q.shape
    dv = v.shape[-1]
    n = s // CHUNK

    def chunks(t):
        return jnp.moveaxis(t.reshape(b, n, CHUNK, h, *t.shape[3:]), 3, 2)

    q = chunks(q) * (dk ** -0.5)
    k, v, g, beta = chunks(k), chunks(v), chunks(g), chunks(beta)
    gc = jnp.cumsum(g, axis=-1)
    tril = jnp.tril(jnp.ones((CHUNK, CHUNK), dtype=bool))
    strict = jnp.tril(jnp.ones((CHUNK, CHUNK), dtype=bool), -1)
    diff = gc[..., :, None] - gc[..., None, :]
    decay = jnp.where(tril, jnp.exp(jnp.where(tril, diff, 0.0)), 0.0)

    kb = k * beta[..., None]
    lower = jnp.where(strict, jnp.einsum('bnhcd,bnhed->bnhce', kb, k) * decay, 0.0)
    a_mat = jnp.eye(CHUNK, dtype=q.dtype) + lower
    rhs = jnp.concatenate([v * beta[..., None], kb * jnp.exp(gc)[..., None]], axis=-1)
    sol = lax.linalg.triangular_solve(a_mat, rhs, left_side=True, lower=True, unit_diagonal=True)
    u, w = sol[..., :dv], sol[..., dv:]

    qk = jnp.where(tril, jnp.einsum('bnhcd,bnhed->bnhce', q, k) * decay, 0.0)
    g_last = gc[..., -1]
    k_dec = k * jnp.exp(g_last[..., None] - gc)[..., None]
    q_dec = q * jnp.exp(gc)[..., None]

    def step(state, xs):
        q_i, qk_i, u_i, w_i, k_i, gl_i = xs
        v_new = u_i - jnp.einsum('bhck,bhkv->bhcv', w_i, state)
        o_i = jnp.einsum('bhck,bhkv->bhcv', q_i, state) + jnp.einsum('bhce,bhev->bhcv', qk_i, v_new)
        state = state * jnp.exp(gl_i)[..., None, None] + jnp.einsum('bhck,bhcv->bhkv', k_i, v_new)
        return state, o_i

    xs = tuple(jnp.moveaxis(t, 1, 0) for t in (q_dec, qk, u, w, k_dec, g_last))
    s0 = jnp.zeros((b, h, dk, dv), dtype=q.dtype)
    _, o = lax.scan(step, s0, xs)
    return jnp.transpose(o, (1, 0, 3, 2, 4)).reshape(b, s, h, dv)

def attention_mixer(hn, w_in, sink, w_out):
    proj = hn @ w_in
    q = proj[..., :A_WIDTH]
    k = proj[..., A_WIDTH:A_WIDTH + A_KV_WIDTH]
    v = proj[..., A_WIDTH + A_KV_WIDTH:A_WIDTH + 2 * A_KV_WIDTH]
    gate = proj[..., A_WIDTH + 2 * A_KV_WIDTH:]
    o = windowed_gqa_sink(q, k, v, sink)
    o = (o * jax.nn.silu(gate.astype(jnp.float32))).astype(hn.dtype)
    return o @ w_out

def deltanet_mixer(hn, w_in, conv_w, a_log, dt_bias, out_norm, w_out):
    b, s, _ = hn.shape
    f32 = jnp.float32
    proj = hn @ w_in
    n_qkv = 2 * B_KW + B_VW
    qkv = jax.nn.silu(short_conv_centred(proj[..., :n_qkv], conv_w)).astype(f32)
    gate = proj[..., n_qkv:n_qkv + B_VW].astype(f32)
    ba = proj[..., n_qkv + B_VW:].astype(f32)
    q = l2_norm(qkv[..., :B_KW].reshape(b, s, B_HEADS, B_HEAD_K))
    k = l2_norm(qkv[..., B_KW:2 * B_KW].reshape(b, s, B_HEADS, B_HEAD_K))
    v = qkv[..., 2 * B_KW:].reshape(b, s, B_HEADS, B_HEAD_V)
    beta = jax.nn.sigmoid(ba[..., :2 * B_HEADS]).reshape(b, s, 2, B_HEADS)
    a = ba[..., 2 * B_HEADS:].reshape(b, s, 2, B_HEADS)
    g = -jnp.exp(a_log.astype(f32)) * jax.nn.softplus(a + dt_bias.astype(f32))

    flip = lambda t: jnp.flip(t, axis=1)
    o_fwd = gated_delta_chunked(q, k, v, g[:, :, 0], beta[:, :, 0])
    o_bwd = flip(gated_delta_chunked(flip(q), flip(k), flip(v), flip(g[:, :, 1]), flip(beta[:, :, 1])))
    o = o_fwd + o_bwd
    o = o * lax.rsqrt(jnp.mean(o * o, axis=-1, keepdims=True) + EPS) * out_norm.astype(f32)
    o = (o.reshape(b, s, B_VW) * jax.nn.silu(gate)).astype(hn.dtype)
    return o @ w_out

def setup_inputs(seed: int = 0) -> dict:
    key = jax.random.key(seed)
    ks = jax.random.split(key, 16)
    f32 = jnp.float32
    nrm = lambda k, shape, scale: jax.random.normal(k, shape, f32) * scale
    dt = jnp.exp(jax.random.uniform(ks[10], (2, B_HEADS), f32, np.log(1e-3), np.log(1e-1)))
    return {
        "x": jax.random.normal(ks[0], (BATCH, SEQ, D_MODEL), f32),
        "attn_norm": 1.0 + nrm(ks[1], (D_MODEL,), 0.02),
        "attn_w_in": nrm(ks[2], (D_MODEL, A_IN), D_MODEL ** -0.5),
        "attn_sink": nrm(ks[3], (A_HEADS,), 0.5),
        "attn_w_out": nrm(ks[4], (A_WIDTH, D_MODEL), A_WIDTH ** -0.5),
        "delta_norm": 1.0 + nrm(ks[5], (D_MODEL,), 0.02),
        "delta_w_in": nrm(ks[6], (D_MODEL, B_IN), D_MODEL ** -0.5),
        "delta_conv": nrm(ks[7], (CONV_WIDTH, 2 * B_KW + B_VW), CONV_WIDTH ** -0.5),
        "delta_a_log": jnp.log(jax.random.uniform(ks[8], (2, B_HEADS), f32, 1.0, 16.0)),
        "delta_dt_bias": dt + jnp.log(-jnp.expm1(-dt)),
        "delta_out_norm": 1.0 + nrm(ks[9], (B_HEAD_V,), 0.02),
        "delta_w_out": nrm(ks[11], (B_VW, D_MODEL), B_VW ** -0.5),
        "final_norm": 1.0 + nrm(ks[12], (D_MODEL,), 0.02),
    }

def reference(x, attn_norm, attn_w_in, attn_sink, attn_w_out,
              delta_norm, delta_w_in, delta_conv, delta_a_log, delta_dt_bias,
              delta_out_norm, delta_w_out, final_norm):
    layer_params = (
        (attn_norm, attn_w_in, attn_sink, attn_w_out),
        (delta_norm, delta_w_in, delta_conv, delta_a_log, delta_dt_bias, delta_out_norm, delta_w_out),
    )
    for i in range(DEPTH):
        p = layer_params[i]
        hn = rms_norm(x, p[0])
        if i % N_MIXERS == 0:
            x = x + attention_mixer(hn, *p[1:])
        else:
            x = x + deltanet_mixer(hn, *p[1:])
    return rms_norm(x, final_norm)


_drawn_inputs = setup_inputs


def setup_inputs(seed=0):
    import zlib

    import numpy as np

    out = dict(_drawn_inputs(seed))
    spreads = {}
    factors = {'attn_norm': 8.0,
     'attn_sink': 5.942,
     'delta_norm': 23.98,
     'delta_out_norm': 40.32,
     'final_norm': 8.338}
    for name, (base, spread) in spreads.items():
        noise = np.random.default_rng([zlib.crc32(name.encode()), seed]).standard_normal(out[name].shape)
        drawn = base * np.exp(spread * noise) if base else spread * noise
        out[name] = __import__('jax').numpy.asarray(drawn.astype(out[name].dtype))
    for name, factor in factors.items():
        out[name] = (out[name] * factor).astype(out[name].dtype)
    return out
```

```python
import concourse.bass as bass
from concourse import mybir
from contextlib import ExitStack

F32 = mybir.dt.float32
I32 = mybir.dt.int32
ALU = mybir.AluOpType
ACT = mybir.ActivationFunctionType
AX = mybir.AxisListType

P = 128
SEQ, D = 1024, 1024
NT = SEQ // P
KT = D // P
HALF = 512
EPS = 1e-6
NEG = -1e30

A_HEADS, A_GROUPS, DH = 16, 4, 64
HPG = A_HEADS // A_GROUPS
W0_TILES = 5
B_HEADS = 8
W1_TILES = 4
LEVELS = 7
PER_HEAD_LINKS = 1 + 12 + 6 + 2 + 3 + 2


def hybrid_encoder_kernel(nc, x, w0, wout0, w1, wba, wout1, norm0, norm1, normf, sink, convw, alog, dtb, onorm, out):
    ctx = ExitStack()
    with ctx:
        def sb(name, shape, dt=F32):
            return ctx.enter_context(nc.sbuf_tensor(name, shape, dt))

        def sem(name):
            return ctx.enter_context(nc.semaphore(name))

        hnT = sb("hnT", [P, KT, SEQ])
        oT = sb("oT", [P, KT, SEQ])
        ident = sb("ident", [P, P])
        g0 = sb("g0", [P, KT])
        g1 = sb("g1", [P, KT])
        onw = sb("onw", [P, 1])
        stat = sb("stat", [P, 6, NT])
        wba_s = sb("wba_s", [P, KT, 32])
        cw = sb("cw", [P, B_HEADS * 15])
        alb = sb("alb", [P, 16])
        dtbb = sb("dtbb", [P, 16])
        ARENA = 36200
        arena = sb("arena", [P, ARENA])
        top = [0]

        def take(shape):
            n = 1
            for s in shape:
                n *= s
            a = arena[:, top[0]:top[0] + n]
            top[0] += n
            assert top[0] <= ARENA, top[0]
            names = "abcdef"[:len(shape)]
            if len(shape) == 1:
                return a
            return a.rearrange(f"p ({' '.join(names)}) -> p {' '.join(names)}",
                               **{c: s for c, s in zip(names[:-1], shape[:-1])})

        ring0 = take([W0_TILES, KT, P])
        xr = take([NT, D])
        wout = take([KT, D])
        qT = take([2, SEQ])
        kz = take([2, SEQ])
        kvT = take([SEQ])
        vtok = kvT.rearrange("p (c e m) -> p c e m", c=NT, e=2)
        gateT0 = take([2, SEQ])
        bias = take([HPG, 3 * P])
        pr = take([2 * HPG, 3 * P])
        pT = take([3, HALF])
        bandm = take([3 * P])
        small0 = take([8 * HPG])
        waited = take([HPG * NT])
        slopes = take([A_HEADS])
        sinkb = take([A_HEADS])
        xn = qT
        distm = take([3 * P])
        disti = pr[:, 0, :].bitcast(I32)
        top[0] = 0
        ring1 = take([W1_TILES, KT, P])
        raw = take([2, SEQ + 4])
        cva = take([3, SEQ])
        inT = take([2, 4, P])
        inX = take([2, 4, P])
        inB = take([2, 4, P])
        kq = take([2, SEQ])
        gateT1 = take([SEQ])
        ktok = take([NT, P])
        vpp = take([NT, P])
        kdec = take([4, P])
        wq = take([2, NT, 2, P])
        invT = take([2, NT, P])
        ET = take([2, NT, P])
        wn = take([2, NT, P])
        S = take([2, P])
        O1 = take([NT, P])
        R = take([2, P])
        lev = take([2, LEVELS, P])
        emask = take([2, P])
        cum = take([2, P])
        gates = take([4, P])
        head_tab = take([10, 16])
        stats1 = take([4, NT])
        junk = take([P])
        gtmp = take([6, P])
        cwh = take([15])
        rq2 = take([NT])
        top[0] = 0
        woutA = take([KT, HALF])
        top[0] = W1_TILES * KT * P
        woutB = take([KT, HALF])
        top[0] = W1_TILES * KT * P + 2 * (SEQ + 4) + 3 * SEQ
        gfb = take([D])
        x1r = take([2, D])
        assert top[0] == W1_TILES * KT * P + 2 * (SEQ + 4) + 3 * SEQ + 3 * 2 * 4 * P
        ytile = take([2, D])
        ysq = take([D])

        bank = [ctx.enter_context(nc.psum_tensor(f"bank{i}", [P, HALF], F32)) for i in range(8)]
        x1_d = nc.dram_tensor("x1_scratch", [P, NT, D], F32).ap()
        gc_d = nc.dram_tensor("gc_scratch", [B_HEADS, 16 * P], F32).ap()

        ld_x = [sem(f"ld_x{t}") for t in range(NT)]
        ld_small = sem("ld_small")
        ld_w = [sem(f"ld_w{i}") for i in range(W0_TILES)]
        ld_v = [sem(f"ld_v{i}") for i in range(W1_TILES)]
        ld_wout = sem("ld_wout")
        ld_wout1 = [sem("ld_wout1a"), sem("ld_wout1b")]
        ld_gf = sem("ld_gf")
        ld_gc = sem("ld_gc")
        ld_x1 = [sem("ld_x1a"), sem("ld_x1b")]
        st_x1 = sem("st_x1")
        st_gc = sem("st_gc")
        st_out = [sem("st_outa"), sem("st_outb")]
        consts = sem("consts")
        kz_zero = sem("kz_zero")
        sq_done = sem("sq_done")
        ms_done = sem("ms_done")
        rt_done = sem("rt_done")
        xn_done = sem("xn_done")
        xT_done = sem("xT_done")
        hn_done = sem("hn_done")
        acc_full = sem("acc_full")
        acc_free = [sem("acc_free0"), sem("acc_free1")]
        kz_done = sem("kz_done")
        s_full = sem("s_full")
        s_masked = sem("s_masked")
        negm_done = sem("negm_done")
        exp_done = sem("exp_done")
        p_norm = sem("p_norm")
        pT_full = sem("pT_full")
        pT_done = sem("pT_done")
        pv_full = sem("pv_full")
        o_done = sem("o_done")
        op_full = sem("op_full")
        x1_half = sem("x1_half")
        ba_full = sem("ba_full")
        ba_act = sem("ba_act")
        ba_dve = sem("ba_dve")
        gc_full = sem("gc_full")
        gc_copied = sem("gc_copied")
        gcT_full = sem("gcT_full")
        gcT_done = sem("gcT_done")
        l1_ready = sem("l1_ready")
        W_full = sem("W_full")
        W_free = [sem("W_free0"), sem("W_free1")]
        raw_done = sem("raw_done")
        conv_done = sem("conv_done")
        silu_done = sem("silu_done")
        ss_done = sem("ss_done")
        tab_dve = sem("tab_dve")
        tab_act = sem("tab_act")
        et_masked = sem("et_masked")
        et_done = sem("et_done")
        bm = [sem("bm0"), sem("bm1")]
        tt_init = [sem("tt_init0"), sem("tt_init1")]
        inv_pe = [sem("inv_pe0"), sem("inv_pe1")]
        invx = [sem("invx0"), sem("invx1")]
        invt = [sem("invt0"), sem("invt1")]
        rec_ks = sem("rec_ks")
        rec_r = sem("rec_r")
        rec_tr = sem("rec_tr")
        rec_w = sem("rec_w")
        rec_kv = sem("rec_kv")
        rec_s = sem("rec_s")
        kdec_done = sem("kdec_done")
        o_sq = sem("o_sq")
        o_ms = sem("o_ms")
        o_fac = sem("o_fac")
        o_nrm = sem("o_nrm")
        fin_full = sem("fin_full")
        fin_add = sem("fin_add")
        fin_sq = sem("fin_sq")
        fin_ms = sem("fin_ms")
        fin_rt = sem("fin_rt")
        fin_y = sem("fin_y")
        dch = sem("dch")
        pch = sem("pch")
        ach = sem("ach")

        def above_zero(value):
            return not isinstance(value, int) or value > 0

        def bc(ap, n, axis=1):
            v = ap.unsqueeze(axis)
            shape = list(v.shape)
            shape[axis] = n
            return v.to_broadcast(shape)

        def key_tiles(n):
            return [k for k in (n - 1, n, n + 1) if 0 <= k < NT]

        def tiles_before(n):
            return sum(len(key_tiles(m)) for m in range(n))
        PT_PER_GROUP = tiles_before(NT)
        A_USES = ([("proj", 0, 0), ("proj", 0, 1), ("proj", 1, 0), ("proj", 1, 1), ("vt", 0, 0), ("vt", 1, 0)]
                  + [("proj", i, hf) for i in (2, 3, 4) for hf in (0, 1)])
        A_HALF_USES = len(A_USES) // 2

        def iteration(first, last):
            ev = []
            rec = [(s, c) for s in range(NT) for c in "abc"]
            if not last:
                for i in range(3):
                    for hf in range(2):
                        for m in range(4):
                            ev.append(("proj", i, hf, m))
                            if not first and rec:
                                ev.append(("rec",) + rec.pop(0))
                    ev.append(("conv", i))
            elif not first:
                ev += [("rec",) + r for r in rec]
            if not first:
                ev += [("osum", 0), ("osum", 1)]
            if not last:
                ev += [("tabs",), ("ktr", 0), ("ktr", 1), ("qtr", 0), ("qtr", 1), ("stab",)]
            if not first:
                ev += [("onorm",)]
            if not last:
                ev += [("vtr", 0), ("vtr", 1)]
            if not first:
                ev += [("otr", 0), ("otr", 1)]
            if not last:
                ev += [("proj", 3, 0, m) for m in range(4)]
                ev += [("gram", 0), ("gram", 1)]
                ev += [("proj", 3, 1, m) for m in range(4)]
                ev += [("gram", 2), ("gram", 3)]
                for rnd in range(2):
                    ev += [("inv0", rnd, 0), ("inv0", rnd, 1)]
                    for lv in range(1, LEVELS):
                        ev += [("invX", rnd, 0, lv), ("invX", rnd, 1, lv), ("invY", rnd, 0, lv), ("invY", rnd, 1, lv)]
            return ev

        def w_index(ev):
            n, idx = 0, {}
            for e in ev:
                if (e[0] == "proj" and e[3] == 0) or e[0] in ("osum", "ktr", "qtr", "vtr", "otr", "gram"):
                    idx[e] = n
                    n += 1
                elif e[0] == "proj":
                    idx[e] = n - 1
            return idx, n
        N_FIRST = w_index(iteration(True, False))[1]
        N_MID = w_index(iteration(False, False))[1]
        W_TOTAL = N_FIRST + (B_HEADS - 1) * N_MID + w_index(iteration(False, True))[1]
        assert N_FIRST % 2 == 0 and N_MID % 2 == 0 and W_TOTAL % 2 == 0

        def w_base(h):
            return 0 if isinstance(h, int) and h == 0 else (h - 1) * N_MID + N_FIRST

        def freed(h, n):
            return n // 2 + 1 if isinstance(h, int) and h == 0 else (h - 1) * (N_MID // 2) + (N_FIRST // 2 + n // 2 + 1)

        def all_freed(h):
            return h * (N_MID // 2) + (N_FIRST - N_MID) // 2

        def unit_group(rnd, p):
            d = p
            lo = 4 * rnd if d == 0 else 4 * (1 - rnd)
            return d, lo

        def first_o1(d, s):
            return s <= 3 or s == NT - 1

        block = ctx.enter_context(nc.Block())

        @block.sync
        def _(sp):
            sp.dma_start(g0[:], norm0).then_inc(ld_small, 16)
            for t in range(NT):
                sp.dma_start(xr[:, t, :], x[:, t, :]).then_inc(ld_x[t], 16)
            for i in range(W0_TILES):
                sp.dma_start(ring0[:, i], w0[0, i]).then_inc(ld_w[i], 16)
            sp.dma_start(sinkb, sink.partition_broadcast(P)).then_inc(ld_small, 16)
            sp.dma_start(g1[:], norm1).then_inc(ld_small, 16)
            sp.dma_start(onw[:], onorm).then_inc(ld_small, 16)
            sp.dma_start(wba_s[:], wba).then_inc(ld_small, 16)
            sp.dma_start(cw[:], convw).then_inc(ld_small, 16)
            sp.dma_start(alb[:], alog.partition_broadcast(P)).then_inc(ld_small, 16)
            sp.dma_start(dtbb[:], dtb.partition_broadcast(P)).then_inc(ld_small, 16)
            sp.dma_start(wout, wout0).then_inc(ld_wout, 16)
            with sp.Fori(1, A_GROUPS) as g:
                for i in range(W0_TILES):
                    sp.wait_ge(acc_full, sp.snap(g * len(A_USES) + (A_USES.index(("proj", i, 1)) + 1 - len(A_USES))))
                    sp.dma_start(ring0[:, i], w0[g, i]).then_inc(ld_w[i], 16)
            for i in range(W1_TILES):
                sp.wait_ge(acc_full, (A_GROUPS - 1) * len(A_USES) + A_USES.index(("proj", i, 1)) + 1)
                sp.dma_start(ring1[:, i], w1[0, i]).then_inc(ld_v[i], 16)
            for t in range(NT):
                sp.wait_ge(x1_half, 2 * t + 2)
                sp.dma_start(x1_d[:, t, :], xr[:, t, :]).then_inc(st_x1, 16)
            sp.wait_ge(gcT_done, 1)
            sp.dma_start(gc_d.rearrange("h (u t) -> (h u) t", t=P), gtmp[:, 0, :]).then_inc(st_gc, 16)
            sp.wait_ge(st_gc, 16)
            sp.dma_start(ET.rearrange("p d c i -> p (d c i)"), gc_d[0].partition_broadcast(P)).then_inc(ld_gc, 16)
            with sp.Fori(1, B_HEADS) as h:
                sp.wait_ge(W_full, sp.snap(w_base(h) - 2))
                for i in range(W1_TILES):
                    sp.dma_start(ring1[:, i], w1[h, i]).then_inc(ld_v[i], 16)
                for b in range(2):
                    sp.wait_ge(W_free[b], sp.snap(all_freed(h)))
                sp.dma_start(ET.rearrange("p d c i -> p (d c i)"), gc_d[h].partition_broadcast(P)).then_inc(ld_gc, 16)
            sp.wait_ge(W_full, w_base(B_HEADS) - 2)
            sp.dma_start(woutA, wout1[:, :, 0:HALF]).then_inc(ld_wout1[0], 16)
            for b in range(2):
                sp.wait_ge(W_free[b], all_freed(B_HEADS))
            sp.dma_start(woutB, wout1[:, :, HALF:D]).then_inc(ld_wout1[1], 16)
            for p in range(2):
                sp.wait_ge(invt[p], B_HEADS * 2 * (LEVELS - 1))
            sp.dma_start(gfb, normf.partition_broadcast(P)).then_inc(ld_gf, 16)
            for t in range(NT):
                if above_zero(2 * (t - 1)):
                    sp.wait_ge(fin_add, 2 * (t - 1))
                sp.dma_start(x1r[:, t % 2], x1_d[:, t, :]).then_inc(ld_x1[t % 2], 16)
                if t >= 1:
                    sp.wait_ge(fin_y, t)
                    sp.dma_start(out[(t - 1) * P:t * P, :], ytile[:, (t - 1) % 2]).then_inc(st_out[(t - 1) % 2], 16)
            sp.wait_ge(fin_y, NT)
            sp.dma_start(out[(NT - 1) * P:NT * P, :], ytile[:, (NT - 1) % 2]).then_inc(st_out[(NT - 1) % 2], 16)
            for b in range(2):
                sp.wait_ge(st_out[b], 16 * (NT // 2))

        @block.gpsimd
        def _(pool):
            gp = nc.gpsimd
            gp.memset(ident[:], 0.0).then_inc(pch, 1)
            gp.memset(bandm, 0.0).then_inc(pch, 1)
            pool.wait_ge(pch, 2)
            gp.affine_select(out=ident[:], in_=ident[:], compare_op=ALU.not_equal, fill=1.0, base=0,
                             pattern=[[-1, P]], channel_multiplier=1).then_inc(consts, 1)
            gp.affine_select(out=bandm, in_=bandm, compare_op=ALU.is_ge, fill=NEG, base=0,
                             pattern=[[1, 3 * P]], channel_multiplier=-1).then_inc(pch, 1)
            pool.wait_ge(pch, 3)
            gp.affine_select(out=bandm, in_=bandm, compare_op=ALU.is_ge, fill=NEG, base=2 * P,
                             pattern=[[-1, 3 * P]], channel_multiplier=1).then_inc(consts, 1)
            gp.iota(disti, pattern=[[1, 3 * P]], base=-P, channel_multiplier=-1).then_inc(consts, 1)
            pool.wait_ge(consts, 3)
            gp.memset(kz[DH:P, 0, :], 0.0).then_inc(kz_zero, 1)
            pool.wait_ge(kz_zero, 1)
            gp.memset(kz[0:DH, 1, :], 0.0).then_inc(kz_zero, 1)
            pool.wait_ge(kz_zero, 2)
            pool.wait_ge(l1_ready, 1)
            for d in range(2):
                gp.memset(emask[:, d], 0.0).then_inc(pch, 1)
                gp.memset(cum[:, d], 1.0).then_inc(pch, 1)
            for j in range(2):
                gp.memset(raw[:, j, 0:2], 0.0)
                gp.memset(raw[:, j, SEQ + 2:SEQ + 4], 0.0).then_inc(consts, 1)
            pool.wait_ge(pch, 7)
            for d in range(2):
                sg = 1 if d == 0 else -1
                gp.affine_select(out=emask[:, d], in_=emask[:, d], compare_op=ALU.is_ge, fill=NEG, base=0,
                                 pattern=[[sg, P]], channel_multiplier=-sg).then_inc(consts, 1)
                gp.affine_select(out=cum[:, d], in_=cum[:, d], compare_op=ALU.is_ge, fill=0.0, base=0,
                                 pattern=[[sg, P]], channel_multiplier=-sg).then_inc(consts, 1)
            gp.iota(gtmp[:, 1].bitcast(I32), pattern=[[1, P]], base=0, channel_multiplier=0).then_inc(consts, 1)
            gp.iota(gtmp[:, 2].bitcast(I32), pattern=[[0, P]], base=0, channel_multiplier=1).then_inc(consts, 1)

            def prepare_and_finish(h, first, last):
                for e in iteration(first, last):
                    if e[0] == "rec" and e[2] == "a" and e[1] < NT - 1:
                        if e[1] == 0:
                            pool.wait_ge(tab_dve, h * 3)
                        for d in range(2):
                            n = 2 * e[1] + d
                            c = e[1] if d == 0 else NT - 1 - e[1]
                            u = 8 * d + c
                            if n >= 4:
                                pool.wait_ge(rec_kv, (h - 1) * 14 + (n - 3))
                            gp.tensor_tensor(kdec[:, n % 4], ktok[:, c], head_tab[:, 4, u:u + 1].to_broadcast([P, P]),
                                             ALU.mult).then_inc(kdec_done, 1)
                    elif e[0] == "tabs":
                        pool.wait_ge(tab_dve, h * 3 + 1)
                        for d in range(2):
                            gp.tensor_tensor(ET[:, d], ET[:, d], bc(emask[:, d], NT), ALU.add).then_inc(et_masked, 1)
                    elif e[0] in ("inv0", "invX"):
                        rnd, p = e[1], e[2]
                        d, lo = unit_group(rnd, p)
                        src = wq[:, d, lo:lo + 4, 0, :]
                        if e[0] == "inv0":
                            if rnd == 0 and p == 0:
                                for b in range(2):
                                    pool.wait_ge(W_free[b], all_freed(h + 1))
                            elif rnd == 1:
                                pool.wait_ge(inv_pe[p], h * 26 + 12)
                            gp.tensor_tensor(inB[:, p], src, bc(lev[:, d, 0], 4), ALU.mult).then_inc(bm[p], 1)
                            pool.wait_ge(tt_init[p], h * 2 + (rnd + 1))
                            gp.tensor_tensor(inB[:, p], src, bc(lev[:, d, 1], 4), ALU.mult).then_inc(bm[p], 1)
                        elif e[3] < LEVELS - 1:
                            pool.wait_ge(inv_pe[p], h * 26 + (13 * rnd + 2 * e[3]))
                            gp.tensor_tensor(inB[:, p], src, bc(lev[:, d, e[3] + 1], 4), ALU.mult).then_inc(bm[p], 1)

            prepare_and_finish(0, True, False)
            with pool.Fori(1, B_HEADS) as h:
                prepare_and_finish(h, False, False)
            prepare_and_finish(B_HEADS, False, True)

        @block.scalar
        def _(act):
            sc = nc.scalar

            def norm_act(t, layer):
                n = NT * layer + t
                if layer == 0:
                    act.wait_ge(ld_x[t], 16)
                else:
                    act.wait_ge(x1_half, 2 * t + 2)
                if above_zero(2 * (n - 1)):
                    act.wait_ge(xT_done, 2 * (n - 1))
                if layer == 1 and t == 0:
                    act.wait_ge(o_done, NT * A_GROUPS + 1)
                sc.activation(xn[:, t % 2], xr[:, t], ACT.Square, accum_out=stat[:, 0, t:t + 1]).then_inc(sq_done, 1)
                act.wait_ge(ms_done, n + 1)
                sc.activation(stat[:, 2, t:t + 1], stat[:, 1, t:t + 1], ACT.Sqrt).then_inc(rt_done, 1)

            for t in range(NT):
                norm_act(t, 0)

            def group(g):
                act.wait_ge(o_done, g * NT + 1)
                for u, (kind, i, hf) in enumerate(A_USES):
                    if kind == "vt":
                        continue
                    act.wait_ge(acc_full, g * len(A_USES) + (u + 1))
                    sl = slice(hf * HALF, (hf + 1) * HALF)
                    if i == 0:
                        ins = sc.activation(kvT[:, sl], bank[u % 2][:], ACT.Copy)
                    elif i <= 2:
                        ins = sc.activation(qT[:, i - 1, sl], bank[u % 2][:], ACT.Copy, scale=DH ** -0.5)
                    else:
                        ins = sc.activation(gateT0[:, i - 3, sl], bank[u % 2][:], ACT.Silu)
                    ins.then_inc(acc_free[u % 2], 1)

                def copy_pT(m):
                    for i in range(len(key_tiles(m))):
                        act.wait_ge(pT_full, g * PT_PER_GROUP + (tiles_before(m) + i + 1))
                        act.wait_ge(pv_full, g * NT + m)
                        sc.activation(pT[:, i], bank[4 + i][:], ACT.Copy).then_inc(pT_done, 1)

                for n in range(NT):
                    act.wait_ge(negm_done, g * NT + (n + 1))
                    w = P * len(key_tiles(n))
                    for hd in range(HPG):
                        sl = (n % 2) * HPG + hd
                        sc.activation(pr[:, sl, 0:w], pr[:, sl, 0:w], ACT.Exp, bias=small0[:, HPG + hd:HPG + hd + 1],
                                      accum_out=small0[:, 3 * HPG + hd:3 * HPG + hd + 1])
                    sc.activation(small0[:, 4 * HPG:5 * HPG], small0[:, 2 * HPG:3 * HPG], ACT.Exp).then_inc(exp_done, 1)
                    if n >= 1:
                        copy_pT(n - 1)
                copy_pT(NT - 1)

            with act.Fori(0, A_GROUPS) as g:
                group(g)

            for t in range(NT):
                norm_act(t, 1)

            act.wait_ge(ba_full, 1)
            act.wait_ge(ld_small, 16 * 8)
            bt = bank[2][:, 0:NT * 32].rearrange("p (c e) -> p c e", e=32)
            beta = gates[:, 0].rearrange("p (h d c) -> p c d h", h=B_HEADS, d=2)
            for d in range(2):
                ins = sc.activation(beta[:, :, d], bt[:, :, 8 * d:8 * d + 8], ACT.Sigmoid)
            ins.then_inc(ba_act, 1)
            act.wait_ge(ba_dve, 1)
            sc.activation(gtmp[:, 2], gtmp[:, 2], ACT.Exp).then_inc(ba_act, 1)
            act.wait_ge(ba_dve, 2)
            sc.activation(gtmp[:, 2], gtmp[:, 2], ACT.Ln).then_inc(ba_act, 1)
            sc.activation(alb[:], alb[:], ACT.Exp).then_inc(ba_act, 1)
            act.wait_ge(gc_copied, 1)
            sc.activation(gates[:, 2], gates[:, 1], ACT.Exp).then_inc(ba_act, 1)

            def prepare_and_finish(h, first, last):
                ev = iteration(first, last)
                idx, _ = w_index(ev)
                wb = w_base(h)

                def full(e):
                    act.wait_ge(W_full, wb + (idx[e] + 1))
                    return bank[idx[e] % 2], W_free[idx[e] % 2]
                for e in ev:
                    if e[0] == "proj" and e[3] == 3:
                        i, hf = e[1], e[2]
                        b, fr = full(e)
                        sl = slice(hf * HALF, (hf + 1) * HALF)
                        if i < 3:
                            if i == 0:
                                if above_zero(h * 3):
                                    act.wait_ge(conv_done, h * 3)
                            elif i == 1:
                                if above_zero(h * 3 - 1):
                                    act.wait_ge(conv_done, h * 3 - 1)
                            else:
                                act.wait_ge(conv_done, h * 3 + 1)
                            sc.activation(raw[:, i % 2, 2 + hf * HALF:2 + (hf + 1) * HALF], b[:], ACT.Copy).then_inc(fr, 1)
                        else:
                            if not first:
                                for j in range(2):
                                    act.wait_ge(W_free[idx[("otr", j)] % 2], freed(h, idx[("otr", j)]))
                            sc.activation(gateT1[:, sl], b[:], ACT.Silu).then_inc(fr, 1)
                    elif e[0] == "rec" and e[2] == "b":
                        for d in range(2):
                            c = e[1] if d == 0 else NT - 1 - e[1]
                            act.wait_ge(rec_tr, (h - 1) * 2 * NT + (2 * e[1] + d + 1))
                            sc.activation(wn[:, d, c], bank[6 + d][:, 2 * P:3 * P], ACT.Copy).then_inc(rec_w, 1)
                    elif e[0] == "osum":
                        act.wait_ge(W_free[idx[e] % 2], freed(h, idx[e]))
                        for c in range(4 * e[1], 4 * e[1] + 4):
                            ins = sc.activation(wn[:, 0, c], O1[:, c], ACT.Square, accum_out=stats1[:, 2, c:c + 1])
                        ins.then_inc(o_sq, 1)
                    elif e[0] == "tabs":
                        act.wait_ge(tab_dve, h * 3 + 1)
                        sc.activation(head_tab[:, 5], head_tab[:, 5], ACT.Exp).then_inc(tab_act, 1)
                        sc.activation(head_tab[:, 6], head_tab[:, 6], ACT.Exp).then_inc(tab_act, 1)
                        for i in range(3):
                            act.wait_ge(conv_done, h * 3 + (i + 1))
                            if i < 2:
                                if not first:
                                    act.wait_ge(rec_ks, (h - 1) * 14 + 14)
                                sc.activation(kq[:, i], cva[:, i], ACT.Silu).then_inc(silu_done, 1)
                            else:
                                sc.activation(cva[:, 2], cva[:, 2], ACT.Silu).then_inc(silu_done, 1)
                    elif e[0] == "ktr":
                        b, fr = full(e)
                        if e[1] == 0 and not first:
                            act.wait_ge(kdec_done, (h - 1) * 14 + 14)
                        sc.activation(ktok[:, 4 * e[1]:4 * e[1] + 4], b.rearrange("p (c k) -> p c k", k=P), ACT.Copy).then_inc(fr, 1)
                        act.wait_ge(fr, freed(h, idx[e]))
                        for c in range(4 * e[1], 4 * e[1] + 4):
                            ins = sc.activation(raw[:, 1, 2 + c * P:2 + (c + 1) * P], ktok[:, c], ACT.Square, accum_out=stats1[:, 0, c:c + 1])
                        ins.then_inc(ss_done, 1)
                    elif e[0] == "qtr":
                        b, fr = full(e)
                        for c in range(4):
                            cc = 4 * e[1] + c
                            ins = sc.activation(raw[:, 0, 2 + cc * P:2 + (cc + 1) * P], b[:, c * P:(c + 1) * P], ACT.Square,
                                                accum_out=stats1[:, 1, cc:cc + 1])
                            if c == 3:
                                ins.then_inc(fr, 1)
                    elif e[0] == "stab":
                        act.wait_ge(tab_dve, h * 3 + 2)
                        sc.activation(head_tab[:, 9, 0:8], head_tab[:, 8, 0:8], ACT.Sqrt).then_inc(tab_act, 1)
                    elif e[0] == "onorm":
                        act.wait_ge(o_ms, h)
                        sc.activation(stats1[:, 3], stats1[:, 3], ACT.Sqrt).then_inc(o_fac, 1)
                    elif e[0] == "vtr" and e[1] == 1:
                        act.wait_ge(et_masked, h * 2 + 2)
                        for d in range(2):
                            for c in range(NT):
                                u = 8 * d + c
                                ins = sc.activation(ET[:, d, c], ET[:, d, c], ACT.Exp, bias=head_tab[:, 2, u:u + 1])
                            ins.then_inc(et_done, 1)
                    elif e[0] == "inv0":
                        rnd, p = e[1], e[2]
                        act.wait_ge(inv_pe[p], h * 26 + (13 * rnd + 1))
                        sc.activation(inT[:, p].rearrange("p c i -> p (c i)"), bank[2 + 2 * p][:], ACT.Copy).then_inc(invx[p], 1)
                    elif e[0] == "invX":
                        rnd, p, lv = e[1], e[2], e[3]
                        act.wait_ge(inv_pe[p], h * 26 + (13 * rnd + 2 * lv))
                        sc.activation(inX[:, p].rearrange("p c i -> p (c i)"), bank[2 + 2 * p][:], ACT.Copy).then_inc(invx[p], 1)

            prepare_and_finish(0, True, False)
            with act.Fori(1, B_HEADS) as h:
                prepare_and_finish(h, False, False)
            prepare_and_finish(B_HEADS, False, True)

            for t in range(NT):
                act.wait_ge(fin_add, 2 * t + 2)
                sc.activation(ysq, ytile[:, t % 2], ACT.Square, accum_out=stat[:, 3, t:t + 1]).then_inc(fin_sq, 1)
                act.wait_ge(fin_ms, t + 1)
                sc.activation(stat[:, 5, t:t + 1], stat[:, 4, t:t + 1], ACT.Sqrt).then_inc(fin_rt, 1)

        @block.vector
        def _(dve):
            ve = nc.vector
            links = [0]

            def link(ins):
                links[0] += 1
                ins.then_inc(dch, 1)
                dve.wait_ge(dch, links[0])

            def norm_dve(t, layer):
                n = NT * layer + t
                dve.wait_ge(sq_done, n + 1)
                ve.tensor_scalar(stat[:, 1, t:t + 1], stat[:, 0, t:t + 1], 1.0 / D, EPS, ALU.mult, ALU.add).then_inc(ms_done, 1)
                dve.wait_ge(rt_done, n + 1)
                link(ve.reciprocal(stat[:, 2, t:t + 1], stat[:, 2, t:t + 1]))
                ve.tensor_scalar(xn[:, t % 2], xr[:, t], stat[:, 2, t:t + 1], None, ALU.mult).then_inc(xn_done, 1)

            def norm_out(t, layer, gain):
                n = NT * layer + t
                for hf in range(2):
                    dve.wait_ge(xT_done, 2 * n + hf + 1)
                    b = bank[4 + 2 * (t % 2) + hf]
                    ve.tensor_tensor(hnT[:, 4 * hf:4 * hf + 4, t * P:(t + 1) * P], b.rearrange("p (k i) -> p k i", i=P),
                                     bc(gain[:, 4 * hf:4 * hf + 4], P, 2), ALU.mult).then_inc(hn_done, 1)

            dve.wait_ge(ld_small, 16 * 8)
            ve.memset(small0[:, 0:16], 0.0).then_inc(acc_free[0], 1)
            ve.memset(small0[:, 16:32], 0.0).then_inc(acc_free[1], 1)
            ve.memset(slopes, 0.0).then_inc(s_masked, 2)
            dve.wait_ge(s_masked, 2)
            for h in range(A_HEADS):
                ins = ve.memset(slopes[:, h:h + 1], -float(2.0 ** (-8.0 * (h + 1) / A_HEADS)))
            ins.then_inc(o_done, 1)
            for t in range(NT):
                norm_dve(t, 0)
                if t >= 1:
                    norm_out(t - 1, 0, g0)
            norm_out(NT - 1, 0, g0)
            dve.wait_ge(consts, 3)
            dve.wait_ge(o_done, 1)
            link(ve.tensor_copy(distm, disti))
            link(ve.tensor_scalar(pr[:, 1], distm, -1.0, None, ALU.mult))
            link(ve.tensor_tensor(distm, distm, pr[:, 1], ALU.max))

            def group(g, base, per):
                k = [0]

                def link(ins):
                    k[0] += 1
                    ins.then_inc(dch, 1)
                    dve.wait_ge(dch, g * per + (base + k[0]))

                link(ve.tensor_scalar(small0[:, 6 * HPG:7 * HPG], slopes[:, bass.ds(g * HPG, HPG)], 1.0, None, ALU.mult))
                link(ve.tensor_scalar(small0[:, 7 * HPG:8 * HPG], sinkb[:, bass.ds(g * HPG, HPG)], 1.0, None, ALU.mult))
                for hd in range(HPG):
                    link(ve.scalar_tensor_tensor(bias[:, hd], distm, small0[:, 6 * HPG + hd:6 * HPG + hd + 1], bandm,
                                                 ALU.mult, ALU.add))
                for u, (kind, i, hf) in enumerate(A_USES):
                    if kind == "vt":
                        dve.wait_ge(acc_full, g * len(A_USES) + (u + 1))
                        dve.wait_ge(kz_done, g * 2 + 2)
                        for e in range(2):
                            ins = ve.tensor_copy(vtok[:, 4 * i:4 * i + 4, e], bank[u % 2].rearrange("p (c m) -> p c m", m=P)[:, :, DH:P])
                        ins.then_inc(acc_free[u % 2], 1)
                    elif i == 0 and hf == 1:
                        dve.wait_ge(acc_free[0], g * A_HALF_USES + 2)
                        dve.wait_ge(acc_free[1], g * A_HALF_USES + 2)
                        ve.tensor_copy(kz[0:DH, 0], kvT[0:DH, :]).then_inc(kz_done, 1)
                        ve.tensor_copy(kz[DH:P, 1], kvT[0:DH, :]).then_inc(kz_done, 1)

                def masked(n, hd):
                    kt = key_tiles(n)
                    w = P * len(kt)
                    off = (kt[0] - n + 1) * P
                    sl = (n % 2) * HPG + hd
                    dve.wait_ge(s_full, g * (HPG * NT) + (HPG * n + hd + 1))
                    ve.memset(waited[:, HPG * n + hd:HPG * n + hd + 1], 0.0)
                    ve.tensor_tensor_reduce(out=pr[:, sl, 0:w], in0=bank[2 + hd % 2][:, 0:w], in1=bias[:, hd, off:off + w],
                                            scale=1.0, scalar=small0[:, 7 * HPG + hd:7 * HPG + hd + 1],
                                            op0=ALU.add, op1=ALU.max,
                                            accum_out=small0[:, hd:hd + 1]).then_inc(s_masked, 1)

                def normalise(n):
                    w = P * len(key_tiles(n))
                    dve.wait_ge(exp_done, g * NT + (n + 1))
                    link(ve.tensor_tensor(small0[:, 5 * HPG:6 * HPG], small0[:, 3 * HPG:4 * HPG], small0[:, 4 * HPG:5 * HPG], ALU.add))
                    link(ve.reciprocal(small0[:, 5 * HPG:6 * HPG], small0[:, 5 * HPG:6 * HPG]))
                    for hd in range(HPG):
                        sl = (n % 2) * HPG + hd
                        ve.tensor_scalar(pr[:, sl, 0:w], pr[:, sl, 0:w], small0[:, 5 * HPG + hd:5 * HPG + hd + 1], None,
                                         ALU.mult).then_inc(p_norm, 1)

                def gated(m):
                    dve.wait_ge(pv_full, g * NT + (m + 1))
                    if m == 0:
                        for b in range(2):
                            dve.wait_ge(acc_free[b], g * A_HALF_USES + (A_HALF_USES + 1))
                    for e in range(2):
                        rows = slice(e * DH, (e + 1) * DH)
                        src = bank[7][rows, :].rearrange("p (j e q) -> p j e q", j=2, e=2)[:, :, e, :]
                        ins = ve.tensor_tensor(oT[rows, bass.ds(g * 2, 2), m * P:(m + 1) * P], src,
                                               gateT0[rows, :, m * P:(m + 1) * P], ALU.mult)
                    ins.then_inc(o_done, 1)

                for n in range(NT):
                    if n >= 1:
                        dve.wait_ge(negm_done, g * NT + n)
                    masked(n, 0)
                    masked(n, 1)
                    if n >= 1:
                        normalise(n - 1)
                    masked(n, 2)
                    masked(n, 3)
                    dve.wait_ge(s_masked, g * (HPG * NT) + (HPG * (n + 1) + 2))
                    ve.tensor_tensor(small0[:, 2 * HPG:3 * HPG], small0[:, 7 * HPG:8 * HPG], small0[:, 0:HPG], ALU.subtract)
                    ve.tensor_scalar(small0[:, HPG:2 * HPG], small0[:, 0:HPG], -1.0, None, ALU.mult).then_inc(negm_done, 1)
                    if n >= 2:
                        gated(n - 2)
                normalise(NT - 1)
                gated(NT - 2)
                gated(NT - 1)
                assert k[0] == per, k[0]

            per = 2 + HPG + 2 * NT
            with dve.Fori(0, A_GROUPS) as g:
                group(g, links[0], per)
            links[0] += per * A_GROUPS

            for t in range(NT):
                for hf in range(2):
                    u = 2 * t + hf
                    dve.wait_ge(op_full, u + 1)
                    sl = slice(hf * HALF, (hf + 1) * HALF)
                    ve.tensor_tensor(xr[:, t, sl], bank[u % 2][:], xr[:, t, sl], ALU.add).then_inc(x1_half, 1)
                if t >= 1:
                    norm_dve(t - 1, 1)
                if t >= 2:
                    norm_out(t - 2, 1, g1)
            norm_dve(NT - 1, 1)
            norm_out(NT - 2, 1, g1)
            norm_out(NT - 1, 1, g1)

            dve.wait_ge(st_x1, 16 * NT)
            ve.memset(junk, 0.0).then_inc(l1_ready, 1)

            dve.wait_ge(consts, 3 + 2 + 4 + 2)
            iv, jv = gtmp[:, 1].bitcast(I32), gtmp[:, 2].bitcast(I32)
            link(ve.tensor_tensor(gtmp[:, 3].bitcast(I32), iv, jv, ALU.bitwise_xor))
            for lv in range(LEVELS):
                link(ve.tensor_scalar(gtmp[:, 4].bitcast(I32), gtmp[:, 3].bitcast(I32), lv, None, ALU.logical_shift_right))
                link(ve.tensor_scalar(gtmp[:, 5], gtmp[:, 4].bitcast(I32), 1.0, None, ALU.is_equal))
                for d in range(2):
                    link(ve.tensor_tensor(lev[:, d, lv], gtmp[:, 5], cum[:, d], ALU.mult))

            dve.wait_ge(ba_full, 1)
            dve.wait_ge(ba_act, 1)
            bt = bank[2][:, 0:NT * 32].rearrange("p (c e) -> p c e", e=32)

            def by_chunk(ap):
                return ap.rearrange("p (c e) -> p c e", e=16)
            link(ve.tensor_tensor(by_chunk(gtmp[:, 1]), bt[:, :, 16:32], bc(dtbb[:], NT), ALU.add))
            link(ve.tensor_scalar(gtmp[:, 2], gtmp[:, 1], -1.0, None, ALU.mult))
            ve.tensor_tensor(gtmp[:, 2], gtmp[:, 2], gtmp[:, 1], ALU.min).then_inc(ba_dve, 1)
            dve.wait_ge(ba_act, 2)
            ve.tensor_scalar(gtmp[:, 2], gtmp[:, 2], 1.0, None, ALU.add).then_inc(ba_dve, 1)
            dve.wait_ge(ba_act, 4)
            link(ve.scalar_tensor_tensor(gtmp[:, 1], gtmp[:, 1], 0.0, gtmp[:, 2], ALU.max, ALU.add))
            for d in range(2):
                ve.scalar_tensor_tensor(gtmp[:, 3].rearrange("p (h d c) -> p d c h", h=B_HEADS, d=2)[:, d],
                                        by_chunk(gtmp[:, 1])[:, :, 8 * d:8 * d + 8], -1.0, bc(alb[:, 8 * d:8 * d + 8], NT),
                                        ALU.mult, ALU.mult).then_inc(ba_dve, 1)
            dve.wait_ge(gc_full, 1)
            ve.tensor_copy(gates[:, 1], bank[3][:, 0:P]).then_inc(gc_copied, 1)
            dve.wait_ge(gc_copied, 1)
            link(ve.tensor_scalar(gates[:, 3], gates[:, 1], -1.0, None, ALU.mult))
            dve.wait_ge(gcT_full, 1)
            ve.tensor_copy(gtmp[:, 0], bank[3][:, P:2 * P]).then_inc(gcT_done, 1)
            dve.wait_ge(ba_act, 5)

            def prepare_and_finish(h, first, last, base, per):
                ev = iteration(first, last)
                idx, _ = w_index(ev)
                wb = w_base(h)
                k = [0]

                def link(ins):
                    k[0] += 1
                    ins.then_inc(dch, 1)
                    dve.wait_ge(dch, (h - 1) * per + (base + k[0]) if per else base + k[0])

                def full(e):
                    dve.wait_ge(W_full, wb + (idx[e] + 1))
                    return bank[idx[e] % 2], W_free[idx[e] % 2]

                def by4(b):
                    return b.rearrange("p (c k) -> p c k", k=P)

                if not last:
                    link(ve.tensor_scalar(cwh, cw[:, 0:15] if first else cw[:, bass.ds(h * 15, 15)], 1.0, None, ALU.mult))
                for e in ev:
                    if e[0] == "conv":
                        i = e[1]
                        for hf in range(2):
                            n = idx[("proj", i, hf, 3)]
                            dve.wait_ge(W_free[n % 2], freed(h, n))
                        if not first:
                            dve.wait_ge(silu_done, h * 3)
                        for j in range(5):
                            tap = cwh[:, i * 5 + j:i * 5 + j + 1]
                            src = raw[:, i % 2, j:j + SEQ]
                            if j == 0:
                                link(ve.tensor_scalar(cva[:, i], src, tap, None, ALU.mult))
                            elif j < 4:
                                link(ve.scalar_tensor_tensor(cva[:, i], src, tap, cva[:, i], ALU.mult, ALU.add))
                            else:
                                ve.scalar_tensor_tensor(cva[:, i], src, tap, cva[:, i], ALU.mult, ALU.add).then_inc(conv_done, 1)
                    elif e[0] == "rec":
                        s, st = e[1], e[2]
                        for d in range(2):
                            c = s if d == 0 else NT - 1 - s
                            u = 8 * d + c
                            b = bank[6 + d]
                            if st == "a" and s > 0:
                                dve.wait_ge(rec_ks, (h - 1) * 14 + (2 * (s - 1) + d + 1))
                                ve.scalar_tensor_tensor(R[:, d], b[:, 0:P], head_tab[:, 1, u:u + 1], vpp[:, c],
                                                        ALU.mult, ALU.add).then_inc(rec_r, 1)
                                eg = head_tab[:, 0, u:u + 1]
                                if first_o1(d, s):
                                    ve.tensor_scalar(O1[:, c], b[:, P:2 * P], eg, None, ALU.mult).then_inc(rec_r, 1)
                                else:
                                    dve.wait_ge(rec_r, (h - 1) * 28 + 4 * (s - 1))
                                    ve.scalar_tensor_tensor(O1[:, c], b[:, P:2 * P], eg, O1[:, c], ALU.mult, ALU.add).then_inc(rec_r, 1)
                            elif st == "c" and s < NT - 1:
                                dve.wait_ge(rec_kv, (h - 1) * 14 + (2 * s + d + 1))
                                if s == 0:
                                    ve.tensor_copy(S[:, d], b[:, 3 * P:4 * P]).then_inc(rec_s, 1)
                                else:
                                    dve.wait_ge(rec_s, (h - 1) * 14 + (2 * (s - 1) + d + 1))
                                    ve.scalar_tensor_tensor(S[:, d], S[:, d], head_tab[:, 5, u:u + 1], b[:, 3 * P:4 * P],
                                                            ALU.mult, ALU.add).then_inc(rec_s, 1)
                    elif e[0] == "osum":
                        b, fr = full(e)
                        dve.wait_ge(rec_r, (h - 1) * 28 + 28)
                        q = slice(4 * e[1], 4 * e[1] + 4)
                        ve.tensor_tensor(O1[:, q], by4(b), O1[:, q], ALU.add).then_inc(fr, 1)
                    elif e[0] == "tabs":
                        dve.wait_ge(ld_gc, h * 16 + 16)
                        if not first:
                            dve.wait_ge(kdec_done, (h - 1) * 14 + 14)
                        for row, (g_row, sign) in enumerate(((2, 1.0), (2, -1.0), (3, 1.0), (0, 1.0))):
                            src = gates[:, g_row, 0:16] if first else gates[:, g_row, bass.ds(h * 16, 16)]
                            link(ve.tensor_scalar(head_tab[:, row], src, sign, None, ALU.mult))
                        link(ve.tensor_copy(head_tab[:, 5, 0:8], ET[:, 0, :, P - 1]))
                        link(ve.tensor_copy(head_tab[:, 5, 8:16], ET[:, 1, :, 0]))
                        ve.tensor_tensor(head_tab[:, 6], head_tab[:, 5], head_tab[:, 2], ALU.add).then_inc(tab_dve, 1)
                    elif e[0] == "stab":
                        dve.wait_ge(ss_done, h * 2 + 2)
                        ve.tensor_scalar(head_tab[:, 8, 0:8], stats1[:, 0], EPS, None, ALU.add).then_inc(tab_dve, 1)
                        dve.wait_ge(tab_dve, h * 3 + 2)
                        link(ve.reciprocal(head_tab[:, 8, 8:16], head_tab[:, 8, 0:8]))
                        link(ve.tensor_tensor(head_tab[:, 7].rearrange("p (d c) -> p d c", d=2),
                                              head_tab[:, 3].rearrange("p (d c) -> p d c", d=2),
                                              bc(head_tab[:, 8, 8:16], 2), ALU.mult))
                        dve.wait_ge(tab_act, h * 3 + 2)
                        ve.tensor_tensor(head_tab[:, 4], head_tab[:, 7], head_tab[:, 6], ALU.mult).then_inc(tab_dve, 1)
                    elif e[0] == "onorm":
                        dve.wait_ge(o_sq, (h - 1) * 2 + 2)
                        link(ve.tensor_tensor(stats1[:, 3], stats1[:, 2], rq2, ALU.mult))
                        link(ve.tensor_scalar(stats1[:, 3], stats1[:, 3], 1.0 / P, EPS, ALU.mult, ALU.add))
                        link(ve.reciprocal(stats1[:, 3], stats1[:, 3]))
                        ve.tensor_tensor(stats1[:, 3], stats1[:, 3], rq2, ALU.mult).then_inc(o_ms, 1)
                        dve.wait_ge(o_fac, h)
                        for j in range(2):
                            q = slice(4 * j, 4 * j + 4)
                            ve.tensor_tensor(O1[:, q], O1[:, q], bc(stats1[:, 3, q], P, 2), ALU.mult).then_inc(o_nrm, 1)
                    elif e[0] == "otr":
                        b, fr = full(e)
                        sl = slice(e[1] * HALF, (e[1] + 1) * HALF)
                        ve.scalar_tensor_tensor(oT[:, h - 1, sl], b[:], onw[:, 0:1], gateT1[:, sl], ALU.mult, ALU.mult).then_inc(fr, 1)
                    elif e[0] == "vtr":
                        b, fr = full(e)
                        if e[1] == 0:
                            for j in range(2):
                                n = idx[("qtr", j)]
                                dve.wait_ge(W_free[n % 2], freed(h, n))
                            link(ve.tensor_scalar(rq2, stats1[:, 1], EPS, float(P), ALU.add, ALU.mult))
                            link(ve.reciprocal(rq2, rq2))
                            dve.wait_ge(tab_act, h * 3 + 3)
                        q = slice(4 * e[1], 4 * e[1] + 4)
                        ve.tensor_tensor(vpp[:, q], by4(b), bc(head_tab[:, 9, q], P, 2), ALU.mult).then_inc(fr, 1)
                    elif e[0] == "gram":
                        b, fr = full(e)
                        dve.wait_ge(et_done, h * 2 + 2)
                        for cc in range(2):
                            c = 2 * e[1] + cc
                            for d in range(2):
                                u = 8 * d + c
                                ins = ve.scalar_tensor_tensor(
                                    wq[:, d, c], b[:, cc * 2 * P:(cc + 1) * 2 * P].rearrange("p (a i) -> p a i", a=2),
                                    head_tab[:, 7, u:u + 1], bc(ET[:, d, c], 2), ALU.mult, ALU.mult)
                        ins.then_inc(fr, 1)
                    elif e[0] == "inv0":
                        rnd, p = e[1], e[2]
                        d, lo = unit_group(rnd, p)
                        dve.wait_ge(bm[p], h * 14 + (7 * rnd + 1))
                        ve.tensor_tensor(invT[:, d, lo:lo + 4], bc(ident[:], 4), inB[:, p], ALU.subtract).then_inc(tt_init[p], 1)
                    elif e[0] == "invY":
                        rnd, p, lv = e[1], e[2], e[3]
                        d, lo = unit_group(rnd, p)
                        dve.wait_ge(inv_pe[p], h * 26 + (13 * rnd + 2 * lv + 1))
                        if lv == 1:
                            dve.wait_ge(tt_init[p], h * 2 + (rnd + 1))
                        else:
                            dve.wait_ge(invt[p], h * 12 + (6 * rnd + lv - 1))
                        if lv < LEVELS - 1:
                            ve.tensor_tensor(inT[:, p], inT[:, p], by4(bank[3 + 2 * p]), ALU.subtract)
                        ve.tensor_tensor(invT[:, d, lo:lo + 4], invT[:, d, lo:lo + 4], by4(bank[2 + 2 * p]), ALU.subtract).then_inc(invt[p], 1)
                return k[0]

            links[0] += prepare_and_finish(0, True, False, links[0], 0)
            per = PER_HEAD_LINKS
            with dve.Fori(1, B_HEADS) as h:
                n = prepare_and_finish(h, False, False, links[0], per)
                assert n == per, n
            links[0] += per * (B_HEADS - 1)
            links[0] += prepare_and_finish(B_HEADS, False, True, links[0], 0)

            dve.wait_ge(ld_gf, 16)
            for t in range(NT):
                dve.wait_ge(ld_x1[t % 2], 16 * (t // 2 + 1))
                if above_zero(16 * (t // 2)):
                    dve.wait_ge(st_out[t % 2], 16 * (t // 2))
                for hf in range(2):
                    sl = slice(hf * HALF, (hf + 1) * HALF)
                    dve.wait_ge(fin_full, 2 * t + hf + 1)
                    ve.tensor_tensor(ytile[:, t % 2, sl], bank[hf][:], x1r[:, t % 2, sl], ALU.add).then_inc(fin_add, 1)
                dve.wait_ge(fin_sq, t + 1)
                ve.tensor_scalar(stat[:, 4, t:t + 1], stat[:, 3, t:t + 1], 1.0 / D, EPS, ALU.mult, ALU.add).then_inc(fin_ms, 1)
                dve.wait_ge(fin_rt, t + 1)
                link(ve.reciprocal(stat[:, 5, t:t + 1], stat[:, 5, t:t + 1]))
                ve.scalar_tensor_tensor(ytile[:, t % 2], ytile[:, t % 2], stat[:, 5, t:t + 1], gfb, ALU.mult, ALU.mult).then_inc(fin_y, 1)

        @block.tensor
        def _(pe):
            te = nc.tensor

            def norm_transposes(t, layer):
                n = NT * layer + t
                pe.wait_ge(xn_done, n + 1)
                for hf in range(2):
                    b = bank[4 + 2 * (t % 2) + hf]
                    if above_zero(2 * (n - 2) + hf + 1):
                        pe.wait_ge(hn_done, 2 * (n - 2) + hf + 1)
                    for k in range(4):
                        ins = te.transpose(b[:, k * P:(k + 1) * P], xn[:, t % 2, (4 * hf + k) * P:(4 * hf + k + 1) * P], ident[:])
                    ins.then_inc(xT_done, 1)

            pe.wait_ge(consts, 3)
            pe.wait_ge(kz_zero, 2)
            for t in range(NT):
                norm_transposes(t, 0)

            def group(g):
                for u, (kind, i, hf) in enumerate(A_USES):
                    b = bank[u % 2]
                    pe.wait_ge(acc_free[u % 2], g * A_HALF_USES + (u // 2 + 1))
                    if kind == "proj":
                        if hf == 0:
                            pe.wait_ge(ld_w[i], g * 16 + 16)
                        if u < 2:
                            pe.wait_ge(hn_done, 2 * NT)
                        for k in range(KT):
                            ins = te.matmul(b[:], ring0[:, i, k], hnT[:, k, hf * HALF:(hf + 1) * HALF],
                                            start=(k == 0), stop=(k == KT - 1))
                    else:
                        if u == 4:
                            for bb in range(2):
                                pe.wait_ge(acc_free[bb], g * A_HALF_USES + 2)
                        for c in range(4):
                            tok = slice((4 * i + c) * P, (4 * i + c + 1) * P)
                            ins = te.transpose(b[:, c * P:(c + 1) * P], kvT[:, tok], ident[:])
                    ins.then_inc(acc_full, 1)

                def logits(n):
                    kt = key_tiles(n)
                    for hd in range(HPG):
                        pe.wait_ge(s_masked, g * (HPG * NT) + (HPG * n + hd + 1))
                        ins = te.matmul(bank[2 + hd % 2][:, 0:P * len(kt)], qT[:, hd // 2, n * P:(n + 1) * P],
                                        kz[:, hd % 2, kt[0] * P:(kt[-1] + 1) * P], start=True, stop=True).then_inc(s_full, 1)

                def transposed(m):
                    if m > 0:
                        pe.wait_ge(pT_done, g * PT_PER_GROUP + tiles_before(m))
                    for i in range(len(key_tiles(m))):
                        for hd in range(HPG):
                            if i == 0:
                                pe.wait_ge(p_norm, g * (HPG * NT) + (HPG * m + hd + 1))
                            ins = te.transpose(bank[4 + i][:, hd * P:(hd + 1) * P],
                                               pr[:, (m % 2) * HPG + hd, i * P:(i + 1) * P], ident[:])
                        ins.then_inc(pT_full, 1)

                def values(m):
                    kt = key_tiles(m)
                    pe.wait_ge(o_done, g * NT + (m + 1))
                    for i, kb in enumerate(kt):
                        pe.wait_ge(pT_done, g * PT_PER_GROUP + (tiles_before(m) + i + 1))
                        ins = te.matmul(bank[7][:], kvT[:, kb * P:(kb + 1) * P], pT[:, i], start=(i == 0), stop=(i == len(kt) - 1))
                    ins.then_inc(pv_full, 1)

                pe.wait_ge(kz_done, g * 2 + 2)
                for b in range(2):
                    pe.wait_ge(acc_free[b], g * A_HALF_USES + 6)
                for n in range(NT):
                    logits(n)
                    if n >= 2:
                        values(n - 2)
                    if n >= 1:
                        transposed(n - 1)
                values(NT - 2)
                transposed(NT - 1)
                values(NT - 1)

            with pe.Fori(0, A_GROUPS) as g:
                group(g)

            pe.wait_ge(ld_wout, 16)
            pe.wait_ge(o_done, A_GROUPS * NT + 1)
            for t in range(NT):
                for hf in range(2):
                    u = 2 * t + hf
                    if above_zero(u - 1):
                        pe.wait_ge(x1_half, u - 1)
                    for j in range(KT):
                        ins = te.matmul(bank[u % 2][:], oT[:, j, t * P:(t + 1) * P], wout[:, j, hf * HALF:(hf + 1) * HALF],
                                        start=(j == 0), stop=(j == KT - 1))
                    ins.then_inc(op_full, 1)
                if t >= 2:
                    norm_transposes(t - 2, 1)
            norm_transposes(NT - 2, 1)
            norm_transposes(NT - 1, 1)

            pe.wait_ge(hn_done, 4 * NT)
            pe.wait_ge(ld_small, 16 * 8)
            for t in range(NT):
                for k in range(KT):
                    ins = te.matmul(bank[2][:, 32 * t:32 * t + 32], hnT[:, k, t * P:(t + 1) * P], wba_s[:, k],
                                    start=(k == 0), stop=(k == KT - 1))
            ins.then_inc(ba_full, 1)
            pe.wait_ge(ba_dve, 4)
            pe.wait_ge(consts, 11)
            gv = gtmp[:, 3].rearrange("p (h d c) -> p h d c", h=B_HEADS, d=2)
            gcv = bank[3][:, 0:P].rearrange("p (h d c) -> p h d c", h=B_HEADS, d=2)
            for d in range(2):
                ins = te.matmul(gcv[:, :, d], cum[:, d], gv[:, :, d], start=True, stop=True)
            ins.then_inc(gc_full, 1)
            pe.wait_ge(gc_copied, 1)
            te.transpose(bank[3][:, P:2 * P], gates[:, 1], ident[:]).then_inc(gcT_full, 1)

            def prepare_and_finish(h, first, last):
                ev = iteration(first, last)
                idx, _ = w_index(ev)

                def work(e):
                    n = idx[e]
                    if not (first and n < 2):
                        pe.wait_ge(W_free[n % 2], freed(h, n) - 1)
                    return bank[n % 2]

                def freed_all(es):
                    for e in es:
                        pe.wait_ge(W_free[idx[e] % 2], freed(h, idx[e]))

                for e in ev:
                    if e[0] == "proj":
                        i, hf, m = e[1], e[2], e[3]
                        if m == 0:
                            b = work(e)
                            if hf == 0:
                                pe.wait_ge(ld_v[i], h * 16 + 16)
                        b = bank[idx[e] % 2]
                        for k in (2 * m, 2 * m + 1):
                            ins = te.matmul(b[:], ring1[:, i, k], hnT[:, k, hf * HALF:(hf + 1) * HALF],
                                            start=(k == 0), stop=(k == KT - 1))
                        if m == 3:
                            ins.then_inc(W_full, 1)
                    elif e[0] == "rec":
                        s, st = e[1], e[2]
                        for d in range(2):
                            c = s if d == 0 else NT - 1 - s
                            b = bank[6 + d]
                            tok = slice(c * P, (c + 1) * P)
                            if st == "a" and s > 0:
                                pe.wait_ge(rec_s, (h - 1) * 14 + (2 * (s - 1) + d + 1))
                                te.matmul(b[:, 0:P], kq[:, 0, tok], S[:, d], start=True, stop=True)
                                te.matmul(b[:, P:2 * P], kq[:, 1, tok], S[:, d], start=True, stop=True).then_inc(rec_ks, 1)
                            elif st == "b":
                                if s > 0:
                                    pe.wait_ge(rec_r, (h - 1) * 28 + (4 * (s - 1) + 2 * d + 2))
                                    rhs = R[:, d]
                                else:
                                    rhs = vpp[:, c]
                                te.matmul(b[:, 2 * P:3 * P], invT[:, d, c], rhs, start=True, stop=True).then_inc(rec_tr, 1)
                            elif st == "c" and s < NT - 1:
                                pe.wait_ge(rec_w, (h - 1) * 16 + (2 * s + d + 1))
                                pe.wait_ge(kdec_done, (h - 1) * 14 + (2 * s + d + 1))
                                te.matmul(b[:, 3 * P:4 * P], kdec[:, (2 * s + d) % 4], wn[:, d, c],
                                          start=True, stop=True).then_inc(rec_kv, 1)
                    elif e[0] == "osum":
                        b = work(e)
                        pe.wait_ge(rec_w, (h - 1) * 16 + 16)
                        for c in range(4):
                            for d in range(2):
                                ins = te.matmul(b[:, c * P:(c + 1) * P], wq[:, d, 4 * e[1] + c, 1], wn[:, d, 4 * e[1] + c],
                                                start=(d == 0), stop=(d == 1))
                        ins.then_inc(W_full, 1)
                    elif e[0] in ("ktr", "qtr", "vtr", "otr"):
                        b = work(e)
                        if e[0] == "otr":
                            pe.wait_ge(o_nrm, (h - 1) * 2 + (e[1] + 1))
                        else:
                            pe.wait_ge(silu_done, h * 3 + {"ktr": 1, "qtr": 2, "vtr": 3}[e[0]])
                        src = {"ktr": kq[:, 0], "qtr": kq[:, 1], "vtr": cva[:, 2], "otr": None}[e[0]]
                        for c in range(4):
                            cc = 4 * e[1] + c
                            piece = O1[:, cc] if e[0] == "otr" else src[:, cc * P:(cc + 1) * P]
                            ins = te.transpose(b[:, c * P:(c + 1) * P], piece, ident[:])
                        ins.then_inc(W_full, 1)
                    elif e[0] == "gram":
                        b = work(e)
                        for cc in range(2):
                            c = 2 * e[1] + cc
                            tok = slice(c * P, (c + 1) * P)
                            ins = te.matmul(b[:, cc * 2 * P:(cc + 1) * 2 * P].rearrange("p (a i) -> p a i", a=2),
                                            kq[:, 0, tok], kq[:, :, tok], start=True, stop=True)
                        ins.then_inc(W_full, 1)
                    elif e[0] == "inv0":
                        rnd, p = e[1], e[2]
                        d, lo = unit_group(rnd, p)
                        pe.wait_ge(tt_init[p], h * 2 + (rnd + 1))
                        if rnd == 1:
                            pe.wait_ge(invt[p], h * 12 + 6)
                        for c in range(4):
                            ins = te.transpose(bank[2 + 2 * p][:, c * P:(c + 1) * P], invT[:, d, lo + c], ident[:])
                        ins.then_inc(inv_pe[p], 1)
                    elif e[0] == "invX":
                        rnd, p, lv = e[1], e[2], e[3]
                        d, lo = unit_group(rnd, p)
                        pe.wait_ge(bm[p], h * 14 + (7 * rnd + lv + 1))
                        pe.wait_ge(invx[p], h * 14 + (7 * rnd + lv))
                        if lv > 1:
                            pe.wait_ge(invt[p], h * 12 + (6 * rnd + lv - 1))
                        for c in range(4):
                            ins = te.matmul(bank[2 + 2 * p][:, c * P:(c + 1) * P], inB[:, p, c], inT[:, p, c], start=True, stop=True)
                        ins.then_inc(inv_pe[p], 1)
                    elif e[0] == "invY":
                        rnd, p, lv = e[1], e[2], e[3]
                        d, lo = unit_group(rnd, p)
                        pe.wait_ge(invx[p], h * 14 + (7 * rnd + lv + 1))
                        for c in range(4):
                            if lv < LEVELS - 1:
                                te.matmul(bank[3 + 2 * p][:, c * P:(c + 1) * P], invT[:, d, lo + c], inX[:, p, c], start=True, stop=True)
                            ins = te.matmul(bank[2 + 2 * p][:, c * P:(c + 1) * P], inX[:, p, c], invT[:, d, lo + c], start=True, stop=True)
                        ins.then_inc(inv_pe[p], 1)

            prepare_and_finish(0, True, False)
            with pe.Fori(1, B_HEADS) as h:
                prepare_and_finish(h, False, False)
            prepare_and_finish(B_HEADS, False, True)

            for b in range(2):
                pe.wait_ge(W_free[b], W_TOTAL // 2)
            for t in range(NT):
                for hf in range(2):
                    pe.wait_ge(ld_wout1[hf], 16)
                    if above_zero(2 * t + hf - 1):
                        pe.wait_ge(fin_add, 2 * t + hf - 1)
                    w = (woutA, woutB)[hf]
                    for j in range(KT):
                        ins = te.matmul(bank[hf][:], oT[:, j, t * P:(t + 1) * P], w[:, j], start=(j == 0), stop=(j == KT - 1))
                    ins.then_inc(fin_full, 1)


def kernel(**inputs):
    import numpy as np
    import concourse.bacc as bacc
    from concourse.bass_utils import run_bass_kernel_spmd

    f = {k: np.asarray(v) for k, v in inputs.items()}

    def tiles(w, starts):
        w3 = w.reshape(KT, P, -1)
        return np.stack([np.concatenate([w3[:, :, a:b] for a, b in cols], axis=2).transpose(1, 0, 2) for cols in starts])

    AW, KW = A_HEADS * DH, A_GROUPS * DH
    w0 = tiles(f["attn_w_in"], [cols for g in range(A_GROUPS) for cols in (
        [(AW + g * DH, AW + (g + 1) * DH), (AW + KW + g * DH, AW + KW + (g + 1) * DH)],
        [(2 * g * P, (2 * g + 1) * P)], [((2 * g + 1) * P, (2 * g + 2) * P)],
        [(AW + 2 * KW + 2 * g * P, AW + 2 * KW + (2 * g + 1) * P)],
        [(AW + 2 * KW + (2 * g + 1) * P, AW + 2 * KW + (2 * g + 2) * P)])]).reshape(A_GROUPS, W0_TILES, P, KT, P)
    BW = B_HEADS * P
    w1 = tiles(f["delta_w_in"], [[(part + h * P, part + (h + 1) * P)] for h in range(B_HEADS)
                                 for part in (BW, 0, 2 * BW, 3 * BW)]).reshape(B_HEADS, W1_TILES, P, KT, P)
    conv = f["delta_conv"].reshape(5, 3, B_HEADS, P)[:, [1, 0, 2]].transpose(3, 2, 1, 0).reshape(P, B_HEADS * 15)
    arrays = {
        "x": f["x"].reshape(NT, P, D).transpose(1, 0, 2),
        "w0": w0,
        "wout0": f["attn_w_out"].reshape(KT, P, D).transpose(1, 0, 2),
        "w1": w1,
        "wba": f["delta_w_in"][:, 4 * BW:].reshape(KT, P, 32).transpose(1, 0, 2),
        "wout1": f["delta_w_out"].reshape(KT, P, D).transpose(1, 0, 2),
        "norm0": f["attn_norm"].reshape(KT, P).T,
        "norm1": f["delta_norm"].reshape(KT, P).T,
        "normf": f["final_norm"],
        "sink": f["attn_sink"],
        "convw": conv,
        "alog": f["delta_a_log"].reshape(16),
        "dtb": f["delta_dt_bias"].reshape(16),
        "onorm": f["delta_out_norm"].reshape(P, 1),
    }
    nc = bacc.Bacc("TRN2", target_bir_lowering=False, num_devices=1)
    sent, args = {}, []
    for name, a in arrays.items():
        sent["in_" + name] = np.ascontiguousarray(a)
        args.append(nc.dram_tensor("in_" + name, a.shape, F32, kind="ExternalInput").ap())
    args.append(nc.dram_tensor("out", (SEQ, D), F32, kind="ExternalOutput").ap())
    hybrid_encoder_kernel(nc, *args)
    r = run_bass_kernel_spmd(nc, [sent], core_ids=[0])
    return r.results[0]["out"].reshape(1, SEQ, D)
```

```python
import concourse.bass as bass
from concourse import mybir
from contextlib import ExitStack

F32 = mybir.dt.float32
F32R = mybir.dt.float32r
I32 = mybir.dt.int32
ALU = mybir.AluOpType
ACT = mybir.ActivationFunctionType
AX = mybir.AxisListType

P = 128
SEQ, D = 1024, 1024
NT = SEQ // P
KT = D // P
HALF = 512
EPS = 1e-6
NEG = -1e30

A_HEADS, A_GROUPS, DH = 16, 4, 64
HPG = A_HEADS // A_GROUPS
W0_TILES = 5
B_HEADS = 8
W1_TILES = 4
FIN_EARLY = 4
LEVELS = 7
XR = 3
PER_HEAD_LINKS = 1 + 12 + 4 + 3 + 2 + 3 + 2


def hybrid_encoder_kernel(nc, x, w0, wout0, w1, wba, wout1, norm0, norm1, normf, sink, convw, alog, dtb, onorm, out):
    ctx = ExitStack()
    with ctx:
        def sb(name, shape, dt=F32):
            return ctx.enter_context(nc.sbuf_tensor(name, shape, dt))

        def sem(name):
            return ctx.enter_context(nc.semaphore(name))

        ident = sb("ident", [P, P])
        g0 = sb("g0", [P, KT])
        g1 = sb("g1", [P, KT])
        onw = sb("onw", [P, 1])
        stat = sb("stat", [P, 6, NT])
        wba_hi = sb("wba_hi", [P, KT, 32], F32R)
        wba_lo = sb("wba_lo", [P, KT, 32], F32R)
        cw = sb("cw", [P, B_HEADS * 15])
        alb = sb("alb", [P, 16])
        dtbb = sb("dtbb", [P, 16])
        ARENA = 52096
        arena_at = nc.sbuf_base
        arena = sb("arena", [P, ARENA])
        top = [0]

        def take(shape):
            n = 1
            for s in shape:
                n *= s
            a = arena[:, top[0]:top[0] + n]
            top[0] += n
            assert top[0] <= ARENA, top[0]
            names = "abcdef"[:len(shape)]
            if len(shape) == 1:
                return a
            return a.rearrange(f"p ({' '.join(names)}) -> p {' '.join(names)}",
                               **{c: s for c, s in zip(names[:-1], shape[:-1])})

        def take_rounded(name, shape):
            t = nc.alloc_sbuf_tensor_at(name, [P] + shape, F32R, offset=arena_at + 4 * top[0])
            take(shape)
            return t

        hn_hi = take_rounded("hn_hi", [KT, SEQ])
        hn_lo = take_rounded("hn_lo", [KT, SEQ])
        HN_END = top[0]
        w0_hi = take_rounded("w0_hi", [2, KT, P])
        w0_lo = take_rounded("w0_lo", [2, KT, P])
        ring0 = take([2, KT, P])
        top[0] = HN_END
        wout = take([KT, D])
        WOUT_END = top[0]
        kz = take([2, SEQ])
        kvT = take([SEQ])
        vtok = kvT.rearrange("p (c e m) -> p c e m", c=NT, e=2)
        gateT0 = take([2, SEQ])
        bias = take([HPG, 3 * P])
        pr_at = top[0]
        pr = take([2 * HPG, 3 * P])
        pT = take([3, HALF])
        wba_s = pT[:, 0, 0:KT * 32].rearrange("p (k e) -> p k e", e=32)
        oT = take([KT, SEQ])
        xr = take([XR, D])
        qT = take([2, SEQ])
        bandm = take([3 * P])
        small0 = take([8 * HPG])
        waited = take([HPG * NT])
        slopes = take([A_HEADS])
        sinkb = take([A_HEADS])
        xn = qT
        distm = take([3 * P])
        disti = pr[:, 0, :].bitcast(I32)
        hn_half = nc.alloc_sbuf_tensor_at("hn_half", [P, 4, 4, P], F32, offset=arena_at + 4 * (pr_at + 2 * 3 * P))
        assert 2 * 3 * P + 4 * HALF <= 2 * HPG * 3 * P
        top[0] = HN_END
        kq = take([2, SEQ])
        gateT1 = take([SEQ])
        ktok = take([NT, P])
        wq = take([2, NT, 2, P])
        assert top[0] == WOUT_END
        w_hi = take_rounded("w_hi", [2, KT, P])
        w_lo = take_rounded("w_lo", [2, KT, P])
        ring1 = take([2, KT, P])
        L1_REST = top[0]
        raw = take([2, SEQ + 4])
        cva = take([3, SEQ])
        inT = take([2, 4, P])
        inX = take([2, 4, P])
        inB = take([2, 4, P])
        vpp = take([NT, P])
        kdec = take([4, P])
        invT = take([2, NT, P])
        ET = take([2, NT, P])
        wn = take([2, NT, P])
        S = take([2, P])
        O1 = take([NT, P])
        baT = O1.rearrange("p c k -> p (c k)")[0:32, :]
        R = take([2, P])
        lev = take([2, LEVELS, P])
        emask = take([2, P])
        cum = take([2, P])
        gates = take([4, P])
        head_tab = take([12, 16])
        stats1 = take([4, NT])
        gtmp = take([6, P])
        cwh = take([15])
        rq2 = take([NT])
        top[0] = 0
        wout_e = take([KT, D])
        oT_e = take([KT, SEQ])
        top[0] = L1_REST + 2 * (SEQ + 4) + 3 * SEQ
        gfb = take([D])
        x1r = take([2, D])
        top[0] = HN_END
        ytile = take([2, D])
        ysq = take([D])

        bank = [ctx.enter_context(nc.psum_tensor(f"bank{i}", [P, HALF], F32)) for i in range(8)]
        x1_d = nc.dram_tensor("x1_scratch", [P, NT, D], F32).ap()
        oT_d = nc.dram_tensor("oT_scratch", [B_HEADS, P, SEQ], F32).ap()
        gc_d = nc.dram_tensor("gc_scratch", [B_HEADS, 16 * P], F32).ap()

        ld_x = [sem(f"ld_x{t}") for t in range(NT)]
        ld_small = sem("ld_small")
        ld_w = [sem(f"ld_w{i}") for i in range(2)]
        w0_rounded = sem("w0_rounded")
        w0_split = sem("w0_split")
        ld_xagain = [sem(f"ld_xagain{t}") for t in range(NT)]
        ld_v = [sem(f"ld_v{i}") for i in range(2)]
        w_rounded = sem("w_rounded")
        w_split = sem("w_split")
        half_done = sem("half_done")
        hi_done = sem("hi_done")
        st_o = sem("st_o")
        ld_oT = sem("ld_oT")
        ld_wout = sem("ld_wout")
        ld_wout1 = sem("ld_wout1")
        ld_gf = sem("ld_gf")
        ld_gc = sem("ld_gc")
        ld_x1 = [sem("ld_x1a"), sem("ld_x1b")]
        st_x1 = sem("st_x1")
        st_gc = sem("st_gc")
        st_out = [sem("st_outa"), sem("st_outb")]
        consts = sem("consts")
        kz_zero = sem("kz_zero")
        sq_done = sem("sq_done")
        ms_done = sem("ms_done")
        rt_done = sem("rt_done")
        xn_done = sem("xn_done")
        xT_done = sem("xT_done")
        hn_done = sem("hn_done")
        acc_full = sem("acc_full")
        acc_free = [sem("acc_free0"), sem("acc_free1")]
        kz_done = sem("kz_done")
        s_full = sem("s_full")
        s_masked = sem("s_masked")
        negm_done = sem("negm_done")
        exp_done = sem("exp_done")
        p_norm = sem("p_norm")
        pT_full = sem("pT_full")
        pT_done = sem("pT_done")
        pv_full = sem("pv_full")
        o_done = sem("o_done")
        op_full = sem("op_full")
        x1_half = sem("x1_half")
        ba_full = sem("ba_full")
        ba_copied = sem("ba_copied")
        ba_tr = sem("ba_tr")
        ba_act = sem("ba_act")
        ba_dve = sem("ba_dve")
        gc_full = sem("gc_full")
        gc_copied = sem("gc_copied")
        gcT_full = sem("gcT_full")
        gcT_done = sem("gcT_done")
        l1_ready = sem("l1_ready")
        W_full = sem("W_full")
        W_free = [sem("W_free0"), sem("W_free1")]
        raw_done = sem("raw_done")
        conv_done = sem("conv_done")
        silu_done = sem("silu_done")
        ss_done = sem("ss_done")
        tab_dve = sem("tab_dve")
        tab_act = sem("tab_act")
        et_masked = sem("et_masked")
        et_done = sem("et_done")
        gram_full = sem("gram_full")
        gram_done = sem("gram_done")
        init_masked = [sem("init_masked0"), sem("init_masked1")]
        tt_init = [sem("tt_init0"), sem("tt_init1")]
        inv_tp = [sem("inv_tp0"), sem("inv_tp1")]
        inT_first = [sem("inT_first0"), sem("inT_first1")]
        bm = [sem("bm0"), sem("bm1")]
        inv_x = [sem("inv_x0"), sem("inv_x1")]
        invx = [sem("invx0"), sem("invx1")]
        inv_y = [sem("inv_y0"), sem("inv_y1")]
        inv_yt = [sem("inv_yt0"), sem("inv_yt1")]
        inT_next = [sem("inT_next0"), sem("inT_next1")]
        invt = [sem("invt0"), sem("invt1")]
        rec_ks = sem("rec_ks")
        rec_r = sem("rec_r")
        rec_tr = sem("rec_tr")
        rec_w = sem("rec_w")
        rec_kv = sem("rec_kv")
        rec_s = sem("rec_s")
        kdec_done = sem("kdec_done")
        o_sq = sem("o_sq")
        o_ms = sem("o_ms")
        o_fac = sem("o_fac")
        o_nrm = sem("o_nrm")
        fin_full = sem("fin_full")
        fin_add = sem("fin_add")
        fin_sq = sem("fin_sq")
        fin_ms = sem("fin_ms")
        fin_rt = sem("fin_rt")
        fin_y = sem("fin_y")
        dch = sem("dch")
        pch = sem("pch")

        def above_zero(value):
            return not isinstance(value, int) or value > 0

        def bc(ap, n, axis=1):
            v = ap.unsqueeze(axis)
            shape = list(v.shape)
            shape[axis] = n
            return v.to_broadcast(shape)

        def key_tiles(n):
            return [k for k in (n - 1, n, n + 1) if 0 <= k < NT]

        def tiles_before(n):
            return sum(len(key_tiles(m)) for m in range(n))
        PT_PER_GROUP = tiles_before(NT)
        A_USES = ([("proj", 0, 0), ("proj", 0, 1), ("proj", 1, 0), ("proj", 1, 1), ("vt", 0, 0), ("vt", 1, 0)]
                  + [("proj", i, hf) for i in (2, 3, 4) for hf in (0, 1)])
        A_HALF_USES = len(A_USES) // 2

        def iteration(first, last):
            ev = []
            rec = [] if first else [("rec", s, c) for s in range(NT) for c in "abc"]
            if last:
                fins = [("fin", u, j) for u in range(FIN_EARLY) for j in range(B_HEADS - 1)]
                ev = []
                for n, r in enumerate(rec):
                    count = 0 if n < 8 else 1 if n < 16 else 2
                    ev += [r] + fins[:count]
                    fins = fins[count:]
                return ev + [("osum", 0), ("osum", 1), ("osq",), ("onorm",)] + fins + [ ("otr", 0), ("otr", 1)]

            def proj(i, hf, ks=range(KT)):
                return [("proj", i, hf, k) for k in ks]
            fill = proj(0, 0) + proj(0, 1) + proj(1, 0) + proj(1, 1) + proj(2, 0)
            side = {1: [("tab1",)], 3: [("etm", 0)], 6: [("etm", 1)],
                    7: [("ete", 0)], 10: [("ete", 1)], 13: [("ete", 2)], 16: [("ete", 3)]}
            for j in range(5):
                side.setdefault(9 + j, []).append(("conv", 0, j))
                side.setdefault(17 + j, []).append(("conv", 1, j))
            side.setdefault(9, []).append(("ws", 2))
            side.setdefault(17, []).append(("ws", 3))
            side[22], side[23] = [("silu", 0)], [("silu", 1)]
            if first:
                del side[3], side[6], side[10], side[16]
                side[1], side[7] = [("gtr",)], [("gcum",)]
                side[9].append(("gctr",))
                side[13] = [("conv", 0, 4), ("tab1",), ("etm", 0), ("etm", 1)]
                side[18].append(("ete", 0))
                side[20] += [("ete", 1), ("ete", 2)]
                side[21] += [("ete", 3)]
                side[23].append(("lev",))
                side[10] = [("conv", 0, 1)]
            for n in range(3 * NT):
                for _ in range(2 if n < 16 else 1):
                    ev.append(fill.pop(0))
                if not first:
                    ev.append(rec[n])
                ev += side.get(n, [])
            if not first:
                ev += [("osum", 0), ("osum", 1)]
            ev += [("tab2",), ("ktr", 0), ("ktr", 1), ("stab",)]
            if not first:
                ev += [("osq",)]
            ev += [("qtr", 0), ("qtr", 1), ("gram", 0), ("gram", 1), ("init", 0, 0)]
            if not first:
                ev += [("onorm",)]
            ev += [("gram", 2), ("gram", 3), ("init", 0, 1)] + proj(2, 1)
            if not first:
                ev += [("otr", 0), ("otr", 1)]
            ev += [("rq",), ("init", 1, 0), ("init", 1, 1)]
            gate = proj(3, 0) + proj(3, 1)
            ev += gate[:5] + [("inv0", 0, 0), ("inv0", 0, 1)]
            fill = gate[5:] + [("vtr", 0), ("vtr", 1)]
            for rnd in range(2):
                if rnd == 1:
                    ev += [("inv0", 1, 0), fill.pop(0), ("inv0", 1, 1)]
                for lv in range(1, LEVELS):
                    ev += [("invX", rnd, 0, lv), ("invX", rnd, 1, lv)]
                    if lv > 1:
                        ev += [("invT", rnd, 0, lv - 1), ("invT", rnd, 1, lv - 1)]
                    ev += [fill.pop(0)]
                    ev += [("invY", rnd, 0, lv), ("invY", rnd, 1, lv)]
                    if rnd == 0 and lv <= 5:
                        ev += [("conv", 2, lv - 1)]
                    if rnd == 0 and lv == LEVELS - 1:
                        ev += [("silu", 2)]
                    if rnd == 0 and lv == 3:
                        ev += [("ws", 0)]
                    if rnd == 1 and lv == 5:
                        ev += [("ws", 1)]
            assert not fill
            return ev

        def w_index(ev):
            n, idx = 0, {}
            for e in ev:
                if (e[0] == "proj" and e[3] == 0) or e[0] in ("osum", "ktr", "qtr", "vtr", "otr"):
                    idx[e] = n
                    n += 1
                elif e[0] == "proj":
                    idx[e] = idx[e[:3] + (0,)]
            return idx, n
        N_FIRST = w_index(iteration(True, False))[1]
        N_MID = w_index(iteration(False, False))[1]
        N_OTR = w_index(iteration(False, False))[0][("otr", 0)]
        def fin_bank(u):
            return bank[2 + u % 4]

        W_TOTAL = N_FIRST + (B_HEADS - 1) * N_MID + w_index(iteration(False, True))[1]
        assert N_FIRST % 2 == 0 and N_MID % 2 == 0 and W_TOTAL % 2 == 0

        def w_base(h):
            return 0 if isinstance(h, int) and h == 0 else (h - 1) * N_MID + N_FIRST

        def freed(h, n):
            return n // 2 + 1 if isinstance(h, int) and h == 0 else (h - 1) * (N_MID // 2) + (N_FIRST // 2 + n // 2 + 1)

        def all_freed(h):
            return h * (N_MID // 2) + (N_FIRST - N_MID) // 2

        def x_bank(p, lv):
            return bank[2 + 2 * p + (lv + 1) % 2]

        def y_bank(p, lv):
            return bank[2 + 2 * p + lv % 2]

        def unit_group(rnd, p):
            d = p
            lo = 4 * rnd if d == 0 else 4 * (1 - rnd)
            return d, lo

        def first_o1(d, s):
            return s <= 3 or s == NT - 1

        block = ctx.enter_context(nc.Block())

        @block.sync
        def _(sp):
            sp.dma_start(g0[:], norm0).then_inc(ld_small, 16)
            for t in range(XR):
                sp.dma_start(xr[:, t, :], x[:, t, :]).then_inc(ld_x[t], 16)
            sp.dma_start(wba_s, wba).then_inc(ld_small, 16)
            for i in range(2):
                sp.dma_start(ring0[:, i], w0[0, i]).then_inc(ld_w[i], 16)
            sp.dma_start(sinkb, sink.partition_broadcast(P)).then_inc(ld_small, 16)
            sp.dma_start(g1[:], norm1).then_inc(ld_small, 16)
            sp.dma_start(onw[:], onorm).then_inc(ld_small, 16)
            sp.dma_start(cw[:], convw).then_inc(ld_small, 16)
            sp.dma_start(alb[:], alog.partition_broadcast(P)).then_inc(ld_small, 16)
            sp.dma_start(dtbb[:], dtb.partition_broadcast(P)).then_inc(ld_small, 16)
            for t in range(XR, NT):
                sp.wait_ge(xn_done, t - XR + 1)
                sp.dma_start(xr[:, t % XR, :], x[:, t, :]).then_inc(ld_x[t], 16)
            for i in range(2, W0_TILES):
                sp.wait_ge(w0_split, i - 1)
                sp.dma_start(ring0[:, i % 2], w0[0, i]).then_inc(ld_w[i % 2], 16)
            with sp.Fori(1, A_GROUPS) as g:
                for i in range(W0_TILES):
                    sp.wait_ge(w0_split, sp.snap(g * W0_TILES + ((i - 1) if i else 0)))
                    sp.dma_start(ring0[:, i % 2], w0[g, i]).then_inc(ld_w[i % 2], 16)
            for i in range(2):
                sp.wait_ge(w0_split, A_GROUPS * W0_TILES)
                sp.dma_start(ring0[:, i], w0[0, i]).then_inc(ld_w[i], 16)
            for t in range(XR):
                sp.dma_start(xr[:, t, :], x[:, t, :]).then_inc(ld_xagain[t], 16)
            sp.wait_ge(w0_split, A_GROUPS * W0_TILES + 2)
            sp.dma_start(wout, wout0).then_inc(ld_wout, 16)
            for i in range(2):
                sp.wait_ge(pv_full, A_GROUPS * NT)
                sp.wait_ge(o_done, A_GROUPS * NT + 1)
                sp.dma_start(ring1[:, i], w1[0, i]).then_inc(ld_v[i], 16)
            for t in range(NT):
                sp.wait_ge(x1_half, 2 * t + 2)
                sp.dma_start(x1_d[:, t, :], xr[:, t % XR, :]).then_inc(st_x1, 16)
                if t + XR < NT:
                    sp.wait_ge(st_x1, 16 * (t + 1))
                    sp.wait_ge(xn_done, NT + t + 1)
                    sp.dma_start(xr[:, t % XR, :], x[:, t + XR, :]).then_inc(ld_xagain[t + XR], 16)
            for i in range(2, W1_TILES):
                sp.wait_ge(w_split, i - 1)
                sp.dma_start(ring1[:, i % 2], w1[0, i]).then_inc(ld_v[i % 2], 16)
            sp.wait_ge(gcT_done, 1)
            sp.dma_start(gc_d.rearrange("h (u t) -> (h u) t", t=P), gtmp[:, 0, :]).then_inc(st_gc, 16)
            sp.wait_ge(st_gc, 16)
            sp.dma_start(ET.rearrange("p d c i -> p (d c i)"), gc_d[0].partition_broadcast(P)).then_inc(ld_gc, 16)
            with sp.Fori(1, B_HEADS) as h:
                for i in range(W1_TILES):
                    if i == 2:
                        sp.wait_ge(gram_done, sp.snap(h * 4))
                        sp.dma_start(ET.rearrange("p d c i -> p (d c i)"), gc_d[h].partition_broadcast(P)).then_inc(ld_gc, 16)
                    sp.wait_ge(w_split, sp.snap(h * 4 + (i - 1)))
                    sp.dma_start(ring1[:, i % 2], w1[h, i]).then_inc(ld_v[i % 2], 16)
                for b in range(2):
                    sp.wait_ge(W_free[b], sp.snap(freed(h, N_OTR + b)))
                sp.dma_start(oT_d[h - 1], gateT1).then_inc(st_o, 16)
            for i in range(2):
                sp.wait_ge(w_split, B_HEADS * 4 + (i - 1))
                sp.dma_start(ring1[:, i], w1[0, i]).then_inc(ld_v[i], 16)
            sp.wait_ge(W_full, w_base(B_HEADS) - 2)
            sp.dma_start(wout_e, wout1).then_inc(ld_wout1, 16)
            sp.wait_ge(st_o, 16 * (B_HEADS - 1))
            sp.dma_start(oT_e[:, 0:B_HEADS - 1], oT_d[0:B_HEADS - 1].rearrange("h p s -> p h s")).then_inc(ld_oT, 16)
            for b in range(2):
                sp.wait_ge(W_free[b], all_freed(B_HEADS))
            for p in range(2):
                sp.wait_ge(invt[p], B_HEADS * 2 * (LEVELS - 1))
            sp.dma_start(gfb, normf.partition_broadcast(P)).then_inc(ld_gf, 16)
            for t in range(NT):
                if above_zero(2 * (t - 1)):
                    sp.wait_ge(fin_add, 2 * (t - 1))
                sp.dma_start(x1r[:, t % 2], x1_d[:, t, :]).then_inc(ld_x1[t % 2], 16)
                if t >= 1:
                    sp.wait_ge(fin_y, t)
                    sp.dma_start(out[(t - 1) * P:t * P, :], ytile[:, (t - 1) % 2]).then_inc(st_out[(t - 1) % 2], 16)
            sp.wait_ge(fin_y, NT)
            sp.dma_start(out[(NT - 1) * P:NT * P, :], ytile[:, (NT - 1) % 2]).then_inc(st_out[(NT - 1) % 2], 16)
            for b in range(2):
                sp.wait_ge(st_out[b], 16 * (NT // 2))

        @block.gpsimd
        def _(pool):
            gp = nc.gpsimd
            gp.memset(ident[:], 0.0).then_inc(pch, 1)
            gp.memset(bandm, 0.0).then_inc(pch, 1)
            pool.wait_ge(pch, 2)
            gp.affine_select(out=ident[:], in_=ident[:], compare_op=ALU.not_equal, fill=1.0, base=0,
                             pattern=[[-1, P]], channel_multiplier=1).then_inc(consts, 1)
            gp.affine_select(out=bandm, in_=bandm, compare_op=ALU.is_ge, fill=NEG, base=0,
                             pattern=[[1, 3 * P]], channel_multiplier=-1).then_inc(pch, 1)
            pool.wait_ge(pch, 3)
            gp.affine_select(out=bandm, in_=bandm, compare_op=ALU.is_ge, fill=NEG, base=2 * P,
                             pattern=[[-1, 3 * P]], channel_multiplier=1).then_inc(consts, 1)
            gp.iota(disti, pattern=[[1, 3 * P]], base=-P, channel_multiplier=-1).then_inc(consts, 1)
            pool.wait_ge(consts, 3)
            gp.memset(kz[DH:P, 0, :], 0.0).then_inc(kz_zero, 1)
            pool.wait_ge(kz_zero, 1)
            gp.memset(kz[0:DH, 1, :], 0.0).then_inc(kz_zero, 1)
            def rest_of_half(t, layer):
                tok = slice(t * P, (t + 1) * P)
                for hf in range(2):
                    q = 2 * (NT * layer + t) + hf
                    ks = slice(4 * hf, 4 * hf + 4)
                    pool.wait_ge(hi_done, q + 1)
                    gp.tensor_tensor(hn_lo[:, ks, tok], hn_half[:, q % 4], hn_hi[:, ks, tok].bitcast(F32),
                                     ALU.subtract).then_inc(hn_done, 1)

            def split0(n, slot):
                pool.wait_ge(w0_rounded, n)
                gp.tensor_tensor(w0_lo[:, slot], ring0[:, slot], w0_hi[:, slot].bitcast(F32), ALU.subtract).then_inc(w0_split, 1)

            for t in range(NT):
                rest_of_half(t, 0)
                if t == 5:
                    split0(1, 0)
            split0(2, 1)
            with pool.Fori(0, A_GROUPS) as g:
                for i in range(2, W0_TILES + 2):
                    split0(g * W0_TILES + (i + 1), i % W0_TILES % 2)
            pool.wait_ge(kz_zero, 2)
            for i in range(2):
                pool.wait_ge(w_rounded, i + 1)
                gp.tensor_tensor(w_lo[:, i], ring1[:, i], w_hi[:, i].bitcast(F32), ALU.subtract).then_inc(w_split, 1)
            for t in range(NT):
                rest_of_half(t, 1)
            pool.wait_ge(l1_ready, 1)
            pool.wait_ge(hn_done, 4 * NT)
            for d in range(2):
                gp.memset(emask[:, d], 0.0).then_inc(pch, 1)
                gp.memset(cum[:, d], 1.0).then_inc(pch, 1)
            for j in range(2):
                gp.memset(raw[:, j, 0:2], 0.0)
                gp.memset(raw[:, j, SEQ + 2:SEQ + 4], 0.0).then_inc(consts, 1)
            pool.wait_ge(pch, 7)
            for d in range(2):
                sg = 1 if d == 0 else -1
                gp.affine_select(out=emask[:, d], in_=emask[:, d], compare_op=ALU.is_ge, fill=NEG, base=0,
                                 pattern=[[sg, P]], channel_multiplier=-sg).then_inc(consts, 1)
                gp.affine_select(out=cum[:, d], in_=cum[:, d], compare_op=ALU.is_ge, fill=0.0, base=0,
                                 pattern=[[sg, P]], channel_multiplier=-sg).then_inc(consts, 1)
            gp.iota(vpp[:, 0].bitcast(I32), pattern=[[1, P]], base=0, channel_multiplier=0).then_inc(consts, 1)
            gp.iota(vpp[:, 1].bitcast(I32), pattern=[[0, P]], base=0, channel_multiplier=1).then_inc(consts, 1)

            def prepare_and_finish(h, first, last):
                for e in iteration(first, last):
                    if e[0] == "rec" and e[2] == "a" and e[1] < NT - 1:
                        if e[1] == 0:
                            pool.wait_ge(tab_dve, h * 3)
                        for d in range(2):
                            n = 2 * e[1] + d
                            c = e[1] if d == 0 else NT - 1 - e[1]
                            u = 8 * d + c
                            if n >= 4:
                                pool.wait_ge(rec_kv, (h - 1) * 14 + (n - 3))
                            gp.tensor_tensor(kdec[:, n % 4], ktok[:, c], head_tab[:, 4, u:u + 1].to_broadcast([P, P]),
                                             ALU.mult).then_inc(kdec_done, 1)
                    elif e[0] == "ws":
                        i = e[1]
                        n = h * 4 + (i + 1 if i >= 2 else i + 5)
                        pool.wait_ge(w_rounded, n)
                        gp.tensor_tensor(w_lo[:, i % 2], ring1[:, i % 2], w_hi[:, i % 2].bitcast(F32), ALU.subtract).then_inc(w_split, 1)
                    elif e[0] == "etm":
                        d = e[1]
                        pool.wait_ge(tab_dve, h * 3 + 1)
                        gp.tensor_tensor(ET[:, d], ET[:, d], bc(emask[:, d], NT), ALU.add).then_inc(et_masked, 1)
                    elif e[0] == "init":
                        rnd, p = e[1], e[2]
                        d, lo = unit_group(rnd, p)
                        src = wq[:, d, lo:lo + 4, 0, :]
                        pool.wait_ge(gram_done, h * 4 + (2 if rnd == 0 and p == 0 else 4))
                        gp.tensor_tensor(invT[:, d, lo:lo + 4], src, bc(lev[:, d, 0], 4), ALU.mult).then_inc(init_masked[p], 1)
                        if rnd == 0:
                            gp.tensor_tensor(inB[:, p], src, bc(lev[:, d, 1], 4), ALU.mult).then_inc(bm[p], 1)
                    elif e[0] in ("inv0", "invX"):
                        rnd, p = e[1], e[2]
                        d, lo = unit_group(rnd, p)
                        src = wq[:, d, lo:lo + 4, 0, :]
                        if e[0] == "inv0" and rnd == 1:
                            pool.wait_ge(inv_x[p], h * 12 + 6)
                            gp.tensor_tensor(inB[:, p], src, bc(lev[:, d, 1], 4), ALU.mult).then_inc(bm[p], 1)
                        elif e[0] == "invX" and e[3] < LEVELS - 1:
                            pool.wait_ge(inv_x[p], h * 12 + (6 * rnd + e[3]))
                            gp.tensor_tensor(inB[:, p], src, bc(lev[:, d, e[3] + 1], 4), ALU.mult).then_inc(bm[p], 1)

            prepare_and_finish(0, True, False)
            with pool.Fori(1, B_HEADS) as h:
                prepare_and_finish(h, False, False)
            prepare_and_finish(B_HEADS, False, True)

        @block.scalar
        def _(act):
            sc = nc.scalar

            def norm_act(t, layer):
                n = NT * layer + t
                if layer == 0:
                    act.wait_ge(ld_x[t], 16)
                else:
                    act.wait_ge(x1_half, 2 * t + 2)
                if above_zero(2 * (n - 1)):
                    act.wait_ge(xT_done, 2 * (n - 1))
                if layer == 1 and t == 0:
                    act.wait_ge(o_done, NT * A_GROUPS + 1)
                sc.activation(xn[:, t % 2], xr[:, t % XR], ACT.Square, accum_out=stat[:, 0, t:t + 1]).then_inc(sq_done, 1)
                act.wait_ge(ms_done, n + 1)
                sc.activation(stat[:, 2, t:t + 1], stat[:, 1, t:t + 1], ACT.Sqrt).then_inc(rt_done, 1)

            def rounded_half(t, layer):
                for hf in range(2):
                    q = 2 * (NT * layer + t) + hf
                    act.wait_ge(half_done, q + 1)
                    sc.activation(hn_hi[:, 4 * hf:4 * hf + 4, t * P:(t + 1) * P], hn_half[:, q % 4], ACT.Copy).then_inc(hi_done, 1)

            for t in range(NT):
                norm_act(t, 0)
                if t >= 2:
                    rounded_half(t - 2, 0)
                if t in (4, 5):
                    act.wait_ge(ld_w[t - 4], 16)
                    sc.activation(w0_hi[:, t - 4], ring0[:, t - 4], ACT.Copy).then_inc(w0_rounded, 1)

            rounded_half(NT - 2, 0)
            rounded_half(NT - 1, 0)

            def group(g):
                def rounded(i):
                    last = {2: 0, 3: 1, 4: 2, 5: 4, 6: 3}[i]
                    slot = i % W0_TILES % 2
                    act.wait_ge(acc_full, g * len(A_USES) + (A_USES.index(("proj", last, 1)) + 1))
                    loads = {2: 2, 3: 2, 4: 3, 5: 4, 6: 3}[i]
                    act.wait_ge(ld_w[slot], g * (16 * (3, 2)[slot]) + 16 * loads)
                    sc.activation(w0_hi[:, slot], ring0[:, slot], ACT.Copy).then_inc(w0_rounded, 1)

                act.wait_ge(o_done, g * NT + 1)
                for u, (kind, i, hf) in enumerate(A_USES):
                    if kind == "vt":
                        continue
                    act.wait_ge(acc_full, g * len(A_USES) + (u + 1))
                    sl = slice(hf * HALF, (hf + 1) * HALF)
                    if i == 0:
                        ins = sc.activation(kvT[:, sl], bank[u % 2][:], ACT.Copy)
                    elif i <= 2:
                        ins = sc.activation(qT[:, i - 1, sl], bank[u % 2][:], ACT.Copy, scale=DH ** -0.5)
                    else:
                        ins = sc.activation(gateT0[:, i - 3, sl], bank[u % 2][:], ACT.Silu)
                    ins.then_inc(acc_free[u % 2], 1)
                    if hf == 1 and i < 3:
                        rounded(i + 2)

                def copy_pT(m):
                    for i in range(len(key_tiles(m))):
                        act.wait_ge(pT_full, g * PT_PER_GROUP + (tiles_before(m) + i + 1))
                        act.wait_ge(pv_full, g * NT + m)
                        sc.activation(pT[:, i], bank[4 + i][:], ACT.Copy).then_inc(pT_done, 1)

                for n in range(NT):
                    act.wait_ge(negm_done, g * NT + (n + 1))
                    w = P * len(key_tiles(n))
                    for hd in range(HPG):
                        sl = (n % 2) * HPG + hd
                        sc.activation(pr[:, sl, 0:w], pr[:, sl, 0:w], ACT.Exp, bias=small0[:, HPG + hd:HPG + hd + 1],
                                      accum_out=small0[:, 3 * HPG + hd:3 * HPG + hd + 1])
                    sc.activation(small0[:, 4 * HPG:5 * HPG], small0[:, 2 * HPG:3 * HPG], ACT.Exp).then_inc(exp_done, 1)
                    if n >= 1:
                        copy_pT(n - 1)
                    if n in (0, 1):
                        rounded(W0_TILES + n)
                copy_pT(NT - 1)

            with act.Fori(0, A_GROUPS) as g:
                group(g)

            act.wait_ge(o_done, A_GROUPS * NT + 1)
            for i in range(2):
                act.wait_ge(ld_v[i], 16)
                sc.activation(w_hi[:, i], ring1[:, i], ACT.Copy).then_inc(w_rounded, 1)
            for t in range(NT):
                norm_act(t, 1)
                if t >= 2:
                    rounded_half(t - 2, 1)
            rounded_half(NT - 2, 1)
            rounded_half(NT - 1, 1)

            act.wait_ge(ba_tr, 1)
            act.wait_ge(ld_small, 16 * 8)
            bt = bank[4][:, 0:NT * 32].rearrange("p (c e) -> p c e", e=32)
            beta = gates[:, 0].rearrange("p (h d c) -> p c d h", h=B_HEADS, d=2)
            for d in range(2):
                ins = sc.activation(beta[:, :, d], bt[:, :, 8 * d:8 * d + 8], ACT.Sigmoid)
            ins.then_inc(ba_act, 1)
            act.wait_ge(ba_dve, 1)
            sc.activation(gtmp[:, 2], gtmp[:, 2], ACT.Exp).then_inc(ba_act, 1)
            act.wait_ge(ba_dve, 2)
            sc.activation(gtmp[:, 2], gtmp[:, 2], ACT.Ln).then_inc(ba_act, 1)
            sc.activation(alb[:], alb[:], ACT.Exp).then_inc(ba_act, 1)
            act.wait_ge(gc_copied, 1)
            sc.activation(gates[:, 2], gates[:, 1], ACT.Exp).then_inc(ba_act, 1)

            def prepare_and_finish(h, first, last):
                ev = iteration(first, last)
                idx, _ = w_index(ev)
                wb = w_base(h)

                def full(e):
                    act.wait_ge(W_full, wb + (idx[e] + 1))
                    return bank[idx[e] % 2], W_free[idx[e] % 2]
                for e in ev:
                    if e[0] == "proj" and e[3] == KT - 1:
                        i, hf = e[1], e[2]
                        b, fr = full(e)
                        sl = slice(hf * HALF, (hf + 1) * HALF)
                        if i < 3:
                            if i == 0:
                                if above_zero(h * 3):
                                    act.wait_ge(conv_done, h * 3)
                            elif i == 1:
                                if above_zero(h * 3 - 1):
                                    act.wait_ge(conv_done, h * 3 - 1)
                            else:
                                act.wait_ge(conv_done, h * 3 + 1)
                            sc.activation(raw[:, i % 2, 2 + hf * HALF:2 + (hf + 1) * HALF], b[:], ACT.Copy).then_inc(fr, 1)
                        else:
                            if not first:
                                act.wait_ge(st_o, h * 16)
                            sc.activation(gateT1[:, sl], b[:], ACT.Silu).then_inc(fr, 1)
                    elif e[0] == "rec" and e[2] == "b":
                        for d in range(2):
                            c = e[1] if d == 0 else NT - 1 - e[1]
                            act.wait_ge(rec_tr, (h - 1) * 2 * NT + (2 * e[1] + d + 1))
                            sc.activation(wn[:, d, c], bank[6 + d][:, 2 * P:3 * P], ACT.Copy).then_inc(rec_w, 1)
                    elif e[0] == "osq":
                        for j in range(2):
                            n = idx[("osum", j)]
                            act.wait_ge(W_free[n % 2], freed(h, n))
                            for c in range(4 * j, 4 * j + 4):
                                ins = sc.activation(wn[:, 0, c], O1[:, c], ACT.Square, accum_out=stats1[:, 2, c:c + 1])
                            ins.then_inc(o_sq, 1)
                    elif e[0] == "ws":
                        i = e[1]
                        last_use = wb + (idx[("proj", (i + 2) % 4, 1, 0)] + 1)
                        act.wait_ge(W_full, last_use)
                        act.wait_ge(ld_v[i % 2], h * 32 + (32 if i >= 2 else 48))
                        sc.activation(w_hi[:, i % 2], ring1[:, i % 2], ACT.Copy).then_inc(w_rounded, 1)
                    elif e[0] == "tab1":
                        act.wait_ge(tab_dve, h * 3 + 1)
                        sc.activation(head_tab[:, 11], head_tab[:, 10], ACT.Exp).then_inc(tab_act, 1)
                        sc.activation(head_tab[:, 6], head_tab[:, 6], ACT.Exp).then_inc(tab_act, 1)
                    elif e[0] == "ete":
                        d, lo = e[1] // 2, 4 * (e[1] % 2)
                        act.wait_ge(et_masked, h * 2 + (d + 1))
                        for c in range(lo, lo + 4):
                            u = 8 * d + c
                            ins = sc.activation(ET[:, d, c], ET[:, d, c], ACT.Exp, bias=head_tab[:, 2, u:u + 1])
                        if lo:
                            ins.then_inc(et_done, 1)
                    elif e[0] == "silu":
                        i = e[1]
                        act.wait_ge(conv_done, h * 3 + (i + 1))
                        if i < 2 and not first:
                            act.wait_ge(rec_ks, (h - 1) * 14 + 14)
                        sc.activation(kq[:, i] if i < 2 else cva[:, 2], cva[:, i], ACT.Silu).then_inc(silu_done, 1)
                    elif e[0] == "ktr":
                        b, fr = full(e)
                        if e[1] == 0 and not first:
                            act.wait_ge(kdec_done, (h - 1) * 14 + 14)
                        sc.activation(ktok[:, 4 * e[1]:4 * e[1] + 4], b.rearrange("p (c k) -> p c k", k=P), ACT.Copy).then_inc(fr, 1)
                    elif e[0] == "qtr":
                        b, fr = full(e)
                        for c in range(4):
                            cc = 4 * e[1] + c
                            ins = sc.activation(cva[:, 1, cc * P:(cc + 1) * P], b[:, c * P:(c + 1) * P], ACT.Square,
                                                accum_out=stats1[:, 1, cc:cc + 1])
                            if c == 3:
                                ins.then_inc(fr, 1)
                    elif e[0] == "stab":
                        for j in range(2):
                            n = idx[("ktr", j)]
                            act.wait_ge(W_free[n % 2], freed(h, n))
                            for c in range(4 * j, 4 * j + 4):
                                ins = sc.activation(cva[:, 0, c * P:(c + 1) * P], ktok[:, c], ACT.Square, accum_out=stats1[:, 0, c:c + 1])
                            ins.then_inc(ss_done, 1)
                        act.wait_ge(tab_dve, h * 3 + 2)
                        sc.activation(head_tab[:, 9, 0:8], head_tab[:, 8, 0:8], ACT.Sqrt).then_inc(tab_act, 1)
                    elif e[0] == "onorm":
                        act.wait_ge(o_ms, h)
                        sc.activation(stats1[:, 3], stats1[:, 3], ACT.Sqrt).then_inc(o_fac, 1)
                    elif e[0] == "inv0":
                        rnd, p = e[1], e[2]
                        act.wait_ge(inv_tp[p], h * 2 + (rnd + 1))
                        if rnd == 1:
                            act.wait_ge(inv_x[p], h * 12 + 6)
                            act.wait_ge(inv_yt[p], h * 10 + 5)
                        sc.activation(inT[:, p].rearrange("p c i -> p (c i)"), x_bank(p, 1)[:], ACT.Copy).then_inc(inT_first[p], 1)
                    elif e[0] == "invX":
                        rnd, p, lv = e[1], e[2], e[3]
                        act.wait_ge(inv_x[p], h * 12 + (6 * rnd + lv))
                        sc.activation(inX[:, p].rearrange("p c i -> p (c i)"), x_bank(p, lv)[:], ACT.Copy).then_inc(invx[p], 1)

            prepare_and_finish(0, True, False)
            with act.Fori(1, B_HEADS) as h:
                prepare_and_finish(h, False, False)
            prepare_and_finish(B_HEADS, False, True)

            for t in range(NT):
                act.wait_ge(fin_add, 2 * t + 2)
                sc.activation(ysq, ytile[:, t % 2], ACT.Square, accum_out=stat[:, 3, t:t + 1]).then_inc(fin_sq, 1)
                act.wait_ge(fin_ms, t + 1)
                sc.activation(stat[:, 5, t:t + 1], stat[:, 4, t:t + 1], ACT.Sqrt).then_inc(fin_rt, 1)

        @block.vector
        def _(dve):
            ve = nc.vector
            links = [0]

            def link(ins):
                links[0] += 1
                ins.then_inc(dch, 1)
                dve.wait_ge(dch, links[0])

            def norm_dve(t, layer):
                n = NT * layer + t
                dve.wait_ge(sq_done, n + 1)
                ve.tensor_scalar(stat[:, 1, t:t + 1], stat[:, 0, t:t + 1], 1.0 / D, EPS, ALU.mult, ALU.add).then_inc(ms_done, 1)
                dve.wait_ge(rt_done, n + 1)
                link(ve.reciprocal(stat[:, 2, t:t + 1], stat[:, 2, t:t + 1]))
                ve.tensor_scalar(xn[:, t % 2], xr[:, t % XR], stat[:, 2, t:t + 1], None, ALU.mult).then_inc(xn_done, 1)

            def norm_out(t, layer, gain):
                n = NT * layer + t
                for hf in range(2):
                    dve.wait_ge(xT_done, 2 * n + hf + 1)
                    b = bank[4 + 2 * (t % 2) + hf]
                    q = 2 * n + hf
                    if q >= 4:
                        dve.wait_ge(hn_done, q - 3)
                    ve.tensor_tensor(hn_half[:, q % 4], b.rearrange("p (k i) -> p k i", i=P),
                                     bc(gain[:, 4 * hf:4 * hf + 4], P, 2), ALU.mult).then_inc(half_done, 1)

            dve.wait_ge(ld_small, 16 * 8)
            link(ve.tensor_copy(wba_hi[:], wba_s))
            link(ve.tensor_tensor(wba_lo[:], wba_s, wba_hi[:].bitcast(F32), ALU.subtract))
            ve.memset(small0[:, 0:16], 0.0).then_inc(acc_free[0], 1)
            ve.memset(small0[:, 16:32], 0.0).then_inc(acc_free[1], 1)
            ve.memset(slopes, 0.0).then_inc(s_masked, 2)
            dve.wait_ge(s_masked, 2)
            for h in range(A_HEADS):
                ins = ve.memset(slopes[:, h:h + 1], -float(2.0 ** (-8.0 * (h + 1) / A_HEADS)))
            ins.then_inc(o_done, 1)
            for t in range(NT):
                norm_dve(t, 0)
                if t >= 1:
                    norm_out(t - 1, 0, g0)
            norm_out(NT - 1, 0, g0)
            dve.wait_ge(consts, 3)
            dve.wait_ge(o_done, 1)
            link(ve.tensor_copy(distm, disti))
            link(ve.tensor_scalar(pr[:, 1], distm, -1.0, None, ALU.mult))
            link(ve.tensor_tensor(distm, distm, pr[:, 1], ALU.max))

            def group(g, base, per):
                k = [0]

                def link(ins):
                    k[0] += 1
                    ins.then_inc(dch, 1)
                    dve.wait_ge(dch, g * per + (base + k[0]))

                link(ve.tensor_scalar(small0[:, 6 * HPG:7 * HPG], slopes[:, bass.ds(g * HPG, HPG)], 1.0, None, ALU.mult))
                link(ve.tensor_scalar(small0[:, 7 * HPG:8 * HPG], sinkb[:, bass.ds(g * HPG, HPG)], 1.0, None, ALU.mult))
                for hd in range(HPG):
                    link(ve.scalar_tensor_tensor(bias[:, hd], distm, small0[:, 6 * HPG + hd:6 * HPG + hd + 1], bandm,
                                                 ALU.mult, ALU.add))
                for u, (kind, i, hf) in enumerate(A_USES):
                    if kind == "vt":
                        dve.wait_ge(acc_full, g * len(A_USES) + (u + 1))
                        dve.wait_ge(kz_done, g * 2 + 2)
                        for e in range(2):
                            ins = ve.tensor_copy(vtok[:, 4 * i:4 * i + 4, e], bank[u % 2].rearrange("p (c m) -> p c m", m=P)[:, :, DH:P])
                        ins.then_inc(acc_free[u % 2], 1)
                    elif i == 0 and hf == 1:
                        dve.wait_ge(acc_free[0], g * A_HALF_USES + 2)
                        dve.wait_ge(acc_free[1], g * A_HALF_USES + 2)
                        ve.tensor_copy(kz[0:DH, 0], kvT[0:DH, :]).then_inc(kz_done, 1)
                        ve.tensor_copy(kz[DH:P, 1], kvT[0:DH, :]).then_inc(kz_done, 1)

                def masked(n, hd):
                    kt = key_tiles(n)
                    w = P * len(kt)
                    off = (kt[0] - n + 1) * P
                    sl = (n % 2) * HPG + hd
                    dve.wait_ge(s_full, g * (HPG * NT) + (HPG * n + hd + 1))
                    ve.memset(waited[:, HPG * n + hd:HPG * n + hd + 1], 0.0)
                    ve.tensor_tensor_reduce(out=pr[:, sl, 0:w], in0=bank[2 + hd % 2][:, 0:w], in1=bias[:, hd, off:off + w],
                                            scale=1.0, scalar=small0[:, 7 * HPG + hd:7 * HPG + hd + 1],
                                            op0=ALU.add, op1=ALU.max,
                                            accum_out=small0[:, hd:hd + 1]).then_inc(s_masked, 1)

                def normalise(n):
                    w = P * len(key_tiles(n))
                    dve.wait_ge(exp_done, g * NT + (n + 1))
                    link(ve.tensor_tensor(small0[:, 5 * HPG:6 * HPG], small0[:, 3 * HPG:4 * HPG], small0[:, 4 * HPG:5 * HPG], ALU.add))
                    link(ve.reciprocal(small0[:, 5 * HPG:6 * HPG], small0[:, 5 * HPG:6 * HPG]))
                    for hd in range(HPG):
                        sl = (n % 2) * HPG + hd
                        ve.tensor_scalar(pr[:, sl, 0:w], pr[:, sl, 0:w], small0[:, 5 * HPG + hd:5 * HPG + hd + 1], None,
                                         ALU.mult).then_inc(p_norm, 1)

                def gated(m):
                    dve.wait_ge(pv_full, g * NT + (m + 1))
                    if m == 0:
                        for b in range(2):
                            dve.wait_ge(acc_free[b], g * A_HALF_USES + (A_HALF_USES + 1))
                    for e in range(2):
                        rows = slice(e * DH, (e + 1) * DH)
                        src = bank[7][rows, :].rearrange("p (j e q) -> p j e q", j=2, e=2)[:, :, e, :]
                        ins = ve.tensor_tensor(oT[rows, bass.ds(g * 2, 2), m * P:(m + 1) * P], src,
                                               gateT0[rows, :, m * P:(m + 1) * P], ALU.mult)
                    ins.then_inc(o_done, 1)

                for n in range(NT):
                    if n >= 1:
                        dve.wait_ge(negm_done, g * NT + n)
                    masked(n, 0)
                    masked(n, 1)
                    if n >= 1:
                        normalise(n - 1)
                    masked(n, 2)
                    masked(n, 3)
                    dve.wait_ge(s_masked, g * (HPG * NT) + (HPG * (n + 1) + 2))
                    ve.tensor_tensor(small0[:, 2 * HPG:3 * HPG], small0[:, 7 * HPG:8 * HPG], small0[:, 0:HPG], ALU.subtract)
                    ve.tensor_scalar(small0[:, HPG:2 * HPG], small0[:, 0:HPG], -1.0, None, ALU.mult).then_inc(negm_done, 1)
                    if n >= 2:
                        gated(n - 2)
                normalise(NT - 1)
                gated(NT - 2)
                gated(NT - 1)
                assert k[0] == per, k[0]

            per = 2 + HPG + 2 * NT
            with dve.Fori(0, A_GROUPS) as g:
                group(g, links[0], per)
            links[0] += per * A_GROUPS

            for t in range(NT):
                for hf in range(2):
                    u = 2 * t + hf
                    dve.wait_ge(op_full, u + 1)
                    sl = slice(hf * HALF, (hf + 1) * HALF)
                    dve.wait_ge(ld_xagain[t], 16)
                    ve.tensor_tensor(xr[:, t % XR, sl], bank[u % 2][:], xr[:, t % XR, sl], ALU.add).then_inc(x1_half, 1)
                if t >= 1:
                    norm_dve(t - 1, 1)
                if t >= 2:
                    norm_out(t - 2, 1, g1)
            norm_dve(NT - 1, 1)
            norm_out(NT - 2, 1, g1)
            norm_out(NT - 1, 1, g1)

            dve.wait_ge(st_x1, 16 * NT)
            ve.memset(rq2, 0.0).then_inc(l1_ready, 1)

            iv, jv = vpp[:, 0].bitcast(I32), vpp[:, 1].bitcast(I32)

            def level_mask(lv, link):
                link(ve.tensor_scalar(vpp[:, 3].bitcast(I32), vpp[:, 2].bitcast(I32), lv, None, ALU.logical_shift_right))
                link(ve.tensor_scalar(vpp[:, 4], vpp[:, 3].bitcast(I32), 1.0, None, ALU.is_equal))
                for d in range(2):
                    link(ve.tensor_tensor(lev[:, d, lv], vpp[:, 4], cum[:, d], ALU.mult))

            for hf in range(2):
                dve.wait_ge(ba_full, hf + 1)
                ve.tensor_copy(baT[:, hf * HALF:(hf + 1) * HALF], bank[2 + hf][0:32, :]).then_inc(ba_copied, 1)
            dve.wait_ge(ba_act, 1)
            bt = bank[4][:, 0:NT * 32].rearrange("p (c e) -> p c e", e=32)

            def by_chunk(ap):
                return ap.rearrange("p (c e) -> p c e", e=16)
            link(ve.tensor_tensor(by_chunk(gtmp[:, 1]), bt[:, :, 16:32], bc(dtbb[:], NT), ALU.add))
            link(ve.tensor_scalar(gtmp[:, 2], gtmp[:, 1], -1.0, None, ALU.mult))
            ve.tensor_tensor(gtmp[:, 2], gtmp[:, 2], gtmp[:, 1], ALU.min).then_inc(ba_dve, 1)
            dve.wait_ge(ba_act, 2)
            ve.tensor_scalar(gtmp[:, 2], gtmp[:, 2], 1.0, None, ALU.add).then_inc(ba_dve, 1)
            dve.wait_ge(ba_act, 4)
            link(ve.scalar_tensor_tensor(gtmp[:, 1], gtmp[:, 1], 0.0, gtmp[:, 2], ALU.max, ALU.add))
            for d in range(2):
                ve.scalar_tensor_tensor(gtmp[:, 3].rearrange("p (h d c) -> p d c h", h=B_HEADS, d=2)[:, d],
                                        by_chunk(gtmp[:, 1])[:, :, 8 * d:8 * d + 8], -1.0, bc(alb[:, 8 * d:8 * d + 8], NT),
                                        ALU.mult, ALU.mult).then_inc(ba_dve, 1)
            dve.wait_ge(consts, 3 + 2 + 4 + 2)
            link(ve.tensor_tensor(vpp[:, 2].bitcast(I32), iv, jv, ALU.bitwise_xor))
            for lv in range(3):
                level_mask(lv, link)
            dve.wait_ge(gc_full, 1)
            ve.tensor_copy(gates[:, 1], bank[3][:, 0:P]).then_inc(gc_copied, 1)
            dve.wait_ge(gc_copied, 1)
            link(ve.tensor_scalar(gates[:, 3], gates[:, 1], -1.0, None, ALU.mult))
            dve.wait_ge(gcT_full, 1)
            ve.tensor_copy(gtmp[:, 0], bank[3][:, P:2 * P]).then_inc(gcT_done, 1)
            dve.wait_ge(ba_act, 5)

            def prepare_and_finish(h, first, last, base, per):
                ev = iteration(first, last)
                idx, _ = w_index(ev)
                wb = w_base(h)
                k = [0]

                def link(ins):
                    k[0] += 1
                    ins.then_inc(dch, 1)
                    dve.wait_ge(dch, (h - 1) * per + (base + k[0]) if per else base + k[0])

                def full(e):
                    dve.wait_ge(W_full, wb + (idx[e] + 1))
                    return bank[idx[e] % 2], W_free[idx[e] % 2]

                def by4(b):
                    return b.rearrange("p (c k) -> p c k", k=P)

                if not last:
                    link(ve.tensor_scalar(cwh, cw[:, 0:15] if first else cw[:, bass.ds(h * 15, 15)], 1.0, None, ALU.mult))
                for e in ev:
                    if e[0] == "lev":
                        for lv in range(3, LEVELS):
                            level_mask(lv, link)
                    elif e[0] == "conv":
                        i, j = e[1], e[2]
                        tap = cwh[:, i * 5 + j:i * 5 + j + 1]
                        src = raw[:, i % 2, j:j + SEQ]
                        if j == 0:
                            for hf in range(2):
                                n = idx[("proj", i, hf, 0)]
                                dve.wait_ge(W_free[n % 2], freed(h, n))
                            if not first:
                                dve.wait_ge(silu_done, h * 3)
                            link(ve.tensor_scalar(cva[:, i], src, tap, None, ALU.mult))
                        elif j < 4:
                            link(ve.scalar_tensor_tensor(cva[:, i], src, tap, cva[:, i], ALU.mult, ALU.add))
                        else:
                            ve.scalar_tensor_tensor(cva[:, i], src, tap, cva[:, i], ALU.mult, ALU.add).then_inc(conv_done, 1)
                    elif e[0] == "rec":
                        s, st = e[1], e[2]
                        for d in range(2):
                            c = s if d == 0 else NT - 1 - s
                            u = 8 * d + c
                            b = bank[6 + d]
                            if st == "a" and s > 0:
                                dve.wait_ge(rec_ks, (h - 1) * 14 + (2 * (s - 1) + d + 1))
                                ve.scalar_tensor_tensor(R[:, d], b[:, 0:P], head_tab[:, 1, u:u + 1], vpp[:, c],
                                                        ALU.mult, ALU.add).then_inc(rec_r, 1)
                                eg = head_tab[:, 0, u:u + 1]
                                if first_o1(d, s):
                                    ve.tensor_scalar(O1[:, c], b[:, P:2 * P], eg, None, ALU.mult).then_inc(rec_r, 1)
                                else:
                                    dve.wait_ge(rec_r, (h - 1) * 28 + 4 * (s - 1))
                                    ve.scalar_tensor_tensor(O1[:, c], b[:, P:2 * P], eg, O1[:, c], ALU.mult, ALU.add).then_inc(rec_r, 1)
                            elif st == "c" and s < NT - 1:
                                dve.wait_ge(rec_kv, (h - 1) * 14 + (2 * s + d + 1))
                                if s == 0:
                                    ve.tensor_copy(S[:, d], b[:, 3 * P:4 * P]).then_inc(rec_s, 1)
                                else:
                                    dve.wait_ge(rec_s, (h - 1) * 14 + (2 * (s - 1) + d + 1))
                                    ve.scalar_tensor_tensor(S[:, d], S[:, d], head_tab[:, 5, u:u + 1], b[:, 3 * P:4 * P],
                                                            ALU.mult, ALU.add).then_inc(rec_s, 1)
                    elif e[0] == "osum":
                        b, fr = full(e)
                        dve.wait_ge(rec_r, (h - 1) * 28 + 28)
                        q = slice(4 * e[1], 4 * e[1] + 4)
                        ve.tensor_tensor(O1[:, q], by4(b), O1[:, q], ALU.add).then_inc(fr, 1)
                    elif e[0] == "tab1":
                        dve.wait_ge(ld_gc, h * 16 + 16)
                        for row, g_row in ((2, 3), (3, 0)):
                            src = gates[:, g_row, 0:16] if first else gates[:, g_row, bass.ds(h * 16, 16)]
                            link(ve.tensor_scalar(head_tab[:, row], src, 1.0, None, ALU.mult))
                        link(ve.tensor_copy(head_tab[:, 10, 0:8], ET[:, 0, :, P - 1]))
                        link(ve.tensor_copy(head_tab[:, 10, 8:16], ET[:, 1, :, 0]))
                        ve.tensor_tensor(head_tab[:, 6], head_tab[:, 10], head_tab[:, 2], ALU.add).then_inc(tab_dve, 1)
                    elif e[0] == "tab2":
                        if not first:
                            dve.wait_ge(kdec_done, (h - 1) * 14 + 14)
                        for row, sign in ((0, 1.0), (1, -1.0)):
                            src = gates[:, 2, 0:16] if first else gates[:, 2, bass.ds(h * 16, 16)]
                            link(ve.tensor_scalar(head_tab[:, row], src, sign, None, ALU.mult))
                        dve.wait_ge(tab_act, h * 3 + 2)
                        link(ve.tensor_copy(head_tab[:, 5], head_tab[:, 11]))
                    elif e[0] == "stab":
                        dve.wait_ge(ss_done, h * 2 + 2)
                        ve.tensor_scalar(head_tab[:, 8, 0:8], stats1[:, 0], EPS, None, ALU.add).then_inc(tab_dve, 1)
                        dve.wait_ge(tab_dve, h * 3 + 2)
                        link(ve.reciprocal(head_tab[:, 8, 8:16], head_tab[:, 8, 0:8]))
                        link(ve.tensor_tensor(head_tab[:, 7].rearrange("p (d c) -> p d c", d=2),
                                              head_tab[:, 3].rearrange("p (d c) -> p d c", d=2),
                                              bc(head_tab[:, 8, 8:16], 2), ALU.mult))
                        ve.tensor_tensor(head_tab[:, 4], head_tab[:, 7], head_tab[:, 6], ALU.mult).then_inc(tab_dve, 1)
                    elif e[0] == "onorm":
                        dve.wait_ge(o_sq, (h - 1) * 2 + 2)
                        link(ve.tensor_tensor(stats1[:, 3], stats1[:, 2], rq2, ALU.mult))
                        link(ve.tensor_scalar(stats1[:, 3], stats1[:, 3], 1.0 / P, EPS, ALU.mult, ALU.add))
                        link(ve.reciprocal(stats1[:, 3], stats1[:, 3]))
                        ve.tensor_tensor(stats1[:, 3], stats1[:, 3], rq2, ALU.mult).then_inc(o_ms, 1)
                        dve.wait_ge(o_fac, h)
                        for j in range(2):
                            q = slice(4 * j, 4 * j + 4)
                            ve.tensor_tensor(O1[:, q], O1[:, q], bc(stats1[:, 3, q], P, 2), ALU.mult).then_inc(o_nrm, 1)
                    elif e[0] == "otr":
                        b, fr = full(e)
                        sl = slice(e[1] * HALF, (e[1] + 1) * HALF)
                        dst = oT_e[:, B_HEADS - 1, sl] if last else gateT1[:, sl]
                        ve.scalar_tensor_tensor(dst, b[:], onw[:, 0:1], gateT1[:, sl], ALU.mult, ALU.mult).then_inc(fr, 1)
                    elif e[0] == "vtr":
                        b, fr = full(e)
                        dve.wait_ge(tab_act, h * 3 + 3)
                        q = slice(4 * e[1], 4 * e[1] + 4)
                        ve.tensor_tensor(vpp[:, q], by4(b), bc(head_tab[:, 9, q], P, 2), ALU.mult).then_inc(fr, 1)
                    elif e[0] == "rq":
                        for j in range(2):
                            n = idx[("qtr", j)]
                            dve.wait_ge(W_free[n % 2], freed(h, n))
                        link(ve.tensor_scalar(rq2, stats1[:, 1], EPS, float(P), ALU.add, ALU.mult))
                        link(ve.reciprocal(rq2, rq2))
                    elif e[0] == "gram":
                        b = bank[2 + e[1]]
                        dve.wait_ge(gram_full, h * 4 + (e[1] + 1))
                        dve.wait_ge(et_done, h * 2 + 2)
                        for cc in range(2):
                            c = 2 * e[1] + cc
                            for d in range(2):
                                u = 8 * d + c
                                ins = ve.scalar_tensor_tensor(
                                    wq[:, d, c], b[:, cc * 2 * P:(cc + 1) * 2 * P].rearrange("p (a i) -> p a i", a=2),
                                    head_tab[:, 7, u:u + 1], bc(ET[:, d, c], 2), ALU.mult, ALU.mult)
                        ins.then_inc(gram_done, 1)
                    elif e[0] == "init":
                        rnd, p = e[1], e[2]
                        d, lo = unit_group(rnd, p)
                        dve.wait_ge(init_masked[p], h * 2 + (rnd + 1))
                        ve.tensor_tensor(invT[:, d, lo:lo + 4], bc(ident[:], 4), invT[:, d, lo:lo + 4], ALU.subtract).then_inc(tt_init[p], 1)
                    elif e[0] == "invY":
                        rnd, p, lv = e[1], e[2], e[3]
                        d, lo = unit_group(rnd, p)
                        dve.wait_ge(inv_y[p], h * 12 + (6 * rnd + lv))
                        if lv < LEVELS - 1:
                            if lv > 1:
                                dve.wait_ge(inT_next[p], h * 10 + (5 * rnd + lv - 1))
                            ve.tensor_tensor(inT[:, p], inT[:, p], by4(y_bank(p, lv)), ALU.subtract).then_inc(inT_next[p], 1)
                        else:
                            dve.wait_ge(invt[p], h * 12 + (6 * rnd + lv - 1))
                            ve.tensor_tensor(invT[:, d, lo:lo + 4], invT[:, d, lo:lo + 4], by4(x_bank(p, lv)), ALU.subtract).then_inc(invt[p], 1)
                    elif e[0] == "invT":
                        rnd, p, lv = e[1], e[2], e[3]
                        d, lo = unit_group(rnd, p)
                        dve.wait_ge(inv_yt[p], h * 10 + (5 * rnd + lv))
                        ve.tensor_copy(invT[:, d, lo:lo + 4], by4(x_bank(p, lv))).then_inc(invt[p], 1)
                return k[0]

            links[0] += prepare_and_finish(0, True, False, links[0], 0)
            per = PER_HEAD_LINKS
            with dve.Fori(1, B_HEADS) as h:
                n = prepare_and_finish(h, False, False, links[0], per)
                assert n == per, n
            links[0] += per * (B_HEADS - 1)
            links[0] += prepare_and_finish(B_HEADS, False, True, links[0], 0)

            dve.wait_ge(ld_gf, 16)
            for t in range(NT):
                dve.wait_ge(ld_x1[t % 2], 16 * (t // 2 + 1))
                if above_zero(16 * (t // 2)):
                    dve.wait_ge(st_out[t % 2], 16 * (t // 2))
                for hf in range(2):
                    sl = slice(hf * HALF, (hf + 1) * HALF)
                    dve.wait_ge(fin_full, 2 * t + hf + 1)
                    ve.tensor_tensor(ytile[:, t % 2, sl], fin_bank(2 * t + hf)[:], x1r[:, t % 2, sl], ALU.add).then_inc(fin_add, 1)
                dve.wait_ge(fin_sq, t + 1)
                ve.tensor_scalar(stat[:, 4, t:t + 1], stat[:, 3, t:t + 1], 1.0 / D, EPS, ALU.mult, ALU.add).then_inc(fin_ms, 1)
                dve.wait_ge(fin_rt, t + 1)
                link(ve.reciprocal(stat[:, 5, t:t + 1], stat[:, 5, t:t + 1]))
                ve.scalar_tensor_tensor(ytile[:, t % 2], ytile[:, t % 2], stat[:, 5, t:t + 1], gfb, ALU.mult, ALU.mult).then_inc(fin_y, 1)

        @block.tensor
        def _(pe):
            te = nc.tensor

            def norm_transposes(t, layer):
                n = NT * layer + t
                pe.wait_ge(xn_done, n + 1)
                for hf in range(2):
                    b = bank[4 + 2 * (t % 2) + hf]
                    if above_zero(2 * (n - 2) + hf + 1):
                        pe.wait_ge(half_done, 2 * (n - 2) + hf + 1)
                    for k in range(4):
                        ins = te.transpose(b[:, k * P:(k + 1) * P], xn[:, t % 2, (4 * hf + k) * P:(4 * hf + k + 1) * P], ident[:])
                    ins.then_inc(xT_done, 1)

            pe.wait_ge(consts, 3)
            pe.wait_ge(kz_zero, 2)
            for t in range(NT):
                norm_transposes(t, 0)

            def group(g):
                for u, (kind, i, hf) in enumerate(A_USES):
                    b = bank[u % 2]
                    pe.wait_ge(acc_free[u % 2], g * A_HALF_USES + (u // 2 + 1))
                    if kind == "proj":
                        if hf == 0:
                            pe.wait_ge(w0_split, g * W0_TILES + (i + 1))
                        if u < 2:
                            pe.wait_ge(hn_done, 2 * NT)
                        for k in range(KT):
                            for m, (wp, hp) in enumerate(((w0_hi, hn_hi), (w0_hi, hn_lo), (w0_lo, hn_hi))):
                                ins = te.matmul(b[:], wp[:, i % 2, k], hp[:, k, hf * HALF:(hf + 1) * HALF],
                                                start=(k == 0 and m == 0), stop=(k == KT - 1 and m == 2))
                    else:
                        if u == 4:
                            for bb in range(2):
                                pe.wait_ge(acc_free[bb], g * A_HALF_USES + 2)
                        for c in range(4):
                            tok = slice((4 * i + c) * P, (4 * i + c + 1) * P)
                            ins = te.transpose(b[:, c * P:(c + 1) * P], kvT[:, tok], ident[:])
                    ins.then_inc(acc_full, 1)

                def logits(n):
                    kt = key_tiles(n)
                    for hd in range(HPG):
                        pe.wait_ge(s_masked, g * (HPG * NT) + (HPG * n + hd + 1))
                        ins = te.matmul(bank[2 + hd % 2][:, 0:P * len(kt)], qT[:, hd // 2, n * P:(n + 1) * P],
                                        kz[:, hd % 2, kt[0] * P:(kt[-1] + 1) * P], start=True, stop=True).then_inc(s_full, 1)

                def transposed(m):
                    if m > 0:
                        pe.wait_ge(pT_done, g * PT_PER_GROUP + tiles_before(m))
                    for i in range(len(key_tiles(m))):
                        for hd in range(HPG):
                            if i == 0:
                                pe.wait_ge(p_norm, g * (HPG * NT) + (HPG * m + hd + 1))
                            ins = te.transpose(bank[4 + i][:, hd * P:(hd + 1) * P],
                                               pr[:, (m % 2) * HPG + hd, i * P:(i + 1) * P], ident[:])
                        ins.then_inc(pT_full, 1)

                def values(m):
                    kt = key_tiles(m)
                    pe.wait_ge(o_done, g * NT + (m + 1))
                    for i, kb in enumerate(kt):
                        pe.wait_ge(pT_done, g * PT_PER_GROUP + (tiles_before(m) + i + 1))
                        ins = te.matmul(bank[7][:], kvT[:, kb * P:(kb + 1) * P], pT[:, i], start=(i == 0), stop=(i == len(kt) - 1))
                    ins.then_inc(pv_full, 1)

                pe.wait_ge(kz_done, g * 2 + 2)
                for b in range(2):
                    pe.wait_ge(acc_free[b], g * A_HALF_USES + 6)
                for n in range(NT):
                    logits(n)
                    if n >= 2:
                        values(n - 2)
                    if n >= 1:
                        transposed(n - 1)
                values(NT - 2)
                transposed(NT - 1)
                values(NT - 1)

            with pe.Fori(0, A_GROUPS) as g:
                group(g)

            def gate_logits(hf):
                pe.wait_ge(hn_done, 2 * NT + NT * (hf + 1))
                for k in range(KT):
                    for m, (wp, hp) in enumerate(((wba_hi, hn_hi), (wba_hi, hn_lo), (wba_lo, hn_hi))):
                        ins = te.matmul(bank[2 + hf][0:32, :], wp[:, k], hp[:, k, hf * HALF:(hf + 1) * HALF],
                                        start=(k == 0 and m == 0), stop=(k == KT - 1 and m == 2))
                ins.then_inc(ba_full, 1)

            pe.wait_ge(ld_wout, 16)
            pe.wait_ge(o_done, A_GROUPS * NT + 1)
            for t in range(NT):
                for hf in range(2):
                    u = 2 * t + hf
                    if above_zero(u - 1):
                        pe.wait_ge(x1_half, u - 1)
                    for j in range(KT):
                        ins = te.matmul(bank[u % 2][:], oT[:, j, t * P:(t + 1) * P], wout[:, j, hf * HALF:(hf + 1) * HALF],
                                        start=(j == 0), stop=(j == KT - 1))
                    ins.then_inc(op_full, 1)
                if t >= 2:
                    norm_transposes(t - 2, 1)
            norm_transposes(NT - 2, 1)
            gate_logits(0)
            norm_transposes(NT - 1, 1)
            gate_logits(1)

            def fin_sum(u, j):
                t, hf = u // 2, u % 2
                if j == 0 and u == 0:
                    pe.wait_ge(ld_wout1, 16)
                    pe.wait_ge(ld_oT, 16)
                if j == 0 and u < 4:
                    pe.wait_ge(invt[u // 2], B_HEADS * 12)
                if j == 0 and u >= 4:
                    pe.wait_ge(fin_add, u - 3)
                return te.matmul(fin_bank(u)[:], oT_e[:, j, t * P:(t + 1) * P], wout_e[:, j, hf * HALF:(hf + 1) * HALF],
                                 start=(j == 0), stop=(j == KT - 1))

            def prepare_and_finish(h, first, last):
                ev = iteration(first, last)
                idx, _ = w_index(ev)

                def work(e):
                    n = idx[e]
                    if not (first and n < 2):
                        pe.wait_ge(W_free[n % 2], freed(h, n) - 1)
                    return bank[n % 2]

                for e in ev:
                    if e[0] == "proj":
                        i, hf, k = e[1], e[2], e[3]
                        if k == 0:
                            work(e)
                            if hf == 0:
                                pe.wait_ge(w_split, h * 4 + (i + 1))
                        b = bank[idx[e] % 2]
                        for m, (wp, hp) in enumerate(((w_hi, hn_hi), (w_hi, hn_lo), (w_lo, hn_hi))):
                            ins = te.matmul(b[:], wp[:, i % 2, k], hp[:, k, hf * HALF:(hf + 1) * HALF],
                                            start=(k == 0 and m == 0), stop=(k == KT - 1 and m == 2))
                        if k == KT - 1:
                            ins.then_inc(W_full, 1)
                    elif e[0] == "fin":
                        fin_sum(e[1], e[2])
                    elif e[0] == "gtr":
                        pe.wait_ge(ba_copied, 2)
                        for t in range(NT):
                            ins = te.transpose(bank[4][:, 32 * t:32 * t + 32], baT[:, t * P:(t + 1) * P], ident[0:32, 0:32])
                        ins.then_inc(ba_tr, 1)
                    elif e[0] == "gcum":
                        pe.wait_ge(ba_dve, 4)
                        pe.wait_ge(consts, 11)
                        gv = gtmp[:, 3].rearrange("p (h d c) -> p h d c", h=B_HEADS, d=2)
                        gcv = bank[3][:, 0:P].rearrange("p (h d c) -> p h d c", h=B_HEADS, d=2)
                        for d in range(2):
                            ins = te.matmul(gcv[:, :, d], cum[:, d], gv[:, :, d], start=True, stop=True)
                        ins.then_inc(gc_full, 1)
                    elif e[0] == "gctr":
                        pe.wait_ge(gc_copied, 1)
                        te.transpose(bank[3][:, P:2 * P], gates[:, 1], ident[:]).then_inc(gcT_full, 1)
                    elif e[0] == "rec":
                        s, st = e[1], e[2]
                        for d in range(2):
                            c = s if d == 0 else NT - 1 - s
                            b = bank[6 + d]
                            tok = slice(c * P, (c + 1) * P)
                            if st == "a" and s > 0:
                                pe.wait_ge(rec_s, (h - 1) * 14 + (2 * (s - 1) + d + 1))
                                te.matmul(b[:, 0:P], kq[:, 0, tok], S[:, d], start=True, stop=True)
                                te.matmul(b[:, P:2 * P], kq[:, 1, tok], S[:, d], start=True, stop=True).then_inc(rec_ks, 1)
                            elif st == "b":
                                if s > 0:
                                    pe.wait_ge(rec_r, (h - 1) * 28 + (4 * (s - 1) + 2 * d + 2))
                                    rhs = R[:, d]
                                else:
                                    if d == 0:
                                        for j in range(2):
                                            pe.wait_ge(W_free[j], all_freed(h))
                                    rhs = vpp[:, c]
                                te.matmul(b[:, 2 * P:3 * P], invT[:, d, c], rhs, start=True, stop=True).then_inc(rec_tr, 1)
                            elif st == "c" and s < NT - 1:
                                pe.wait_ge(rec_w, (h - 1) * 16 + (2 * s + d + 1))
                                pe.wait_ge(kdec_done, (h - 1) * 14 + (2 * s + d + 1))
                                te.matmul(b[:, 3 * P:4 * P], kdec[:, (2 * s + d) % 4], wn[:, d, c],
                                          start=True, stop=True).then_inc(rec_kv, 1)
                    elif e[0] == "osum":
                        b = work(e)
                        pe.wait_ge(rec_w, (h - 1) * 16 + 16)
                        for c in range(4):
                            for d in range(2):
                                ins = te.matmul(b[:, c * P:(c + 1) * P], wq[:, d, 4 * e[1] + c, 1], wn[:, d, 4 * e[1] + c],
                                                start=(d == 0), stop=(d == 1))
                        ins.then_inc(W_full, 1)
                    elif e[0] in ("ktr", "qtr", "vtr", "otr"):
                        b = work(e)
                        if e[0] == "otr":
                            pe.wait_ge(o_nrm, (h - 1) * 2 + (e[1] + 1))
                        else:
                            pe.wait_ge(silu_done, h * 3 + {"ktr": 1, "qtr": 2, "vtr": 3}[e[0]])
                        src = {"ktr": kq[:, 0], "qtr": kq[:, 1], "vtr": cva[:, 2], "otr": None}[e[0]]
                        for c in range(4):
                            cc = 4 * e[1] + c
                            piece = O1[:, cc] if e[0] == "otr" else src[:, cc * P:(cc + 1) * P]
                            ins = te.transpose(b[:, c * P:(c + 1) * P], piece, ident[:])
                        ins.then_inc(W_full, 1)
                    elif e[0] == "gram":
                        b = bank[2 + e[1]]
                        pe.wait_ge(silu_done, h * 3 + 2)
                        if first:
                            pe.wait_ge(gcT_done, 1)
                        else:
                            pe.wait_ge(invt[e[1] // 2], h * 12)
                        for cc in range(2):
                            c = 2 * e[1] + cc
                            tok = slice(c * P, (c + 1) * P)
                            ins = te.matmul(b[:, cc * 2 * P:(cc + 1) * 2 * P].rearrange("p (a i) -> p a i", a=2),
                                            kq[:, 0, tok], kq[:, :, tok], start=True, stop=True)
                        ins.then_inc(gram_full, 1)
                    elif e[0] == "inv0":
                        rnd, p = e[1], e[2]
                        d, lo = unit_group(rnd, p)
                        pe.wait_ge(tt_init[p], h * 2 + (rnd + 1))
                        if rnd == 1:
                            pe.wait_ge(invt[p], h * 12 + 5)
                        for c in range(4):
                            ins = te.transpose(x_bank(p, 1)[:, c * P:(c + 1) * P], invT[:, d, lo + c], ident[:])
                        ins.then_inc(inv_tp[p], 1)
                    elif e[0] == "invX":
                        rnd, p, lv = e[1], e[2], e[3]
                        pe.wait_ge(bm[p], h * 12 + (6 * rnd + lv))
                        if lv == 1:
                            pe.wait_ge(inT_first[p], h * 2 + (rnd + 1))
                        else:
                            pe.wait_ge(inT_next[p], h * 10 + (5 * rnd + lv - 1))
                        for c in range(4):
                            ins = te.matmul(x_bank(p, lv)[:, c * P:(c + 1) * P], inB[:, p, c], inT[:, p, c], start=True, stop=True)
                        ins.then_inc(inv_x[p], 1)
                    elif e[0] == "invY":
                        rnd, p, lv = e[1], e[2], e[3]
                        d, lo = unit_group(rnd, p)
                        pe.wait_ge(invx[p], h * 12 + (6 * rnd + lv))
                        if lv > 1:
                            pe.wait_ge(invt[p], h * 12 + (6 * rnd + lv - 1))
                        elif rnd:
                            pe.wait_ge(invt[p], h * 12 + 6)
                        for c in range(4):
                            if lv < LEVELS - 1:
                                ins = te.matmul(y_bank(p, lv)[:, c * P:(c + 1) * P], invT[:, d, lo + c], inX[:, p, c], start=True, stop=True)
                            else:
                                ins = te.matmul(x_bank(p, lv)[:, c * P:(c + 1) * P], inX[:, p, c], invT[:, d, lo + c], start=True, stop=True)
                        ins.then_inc(inv_y[p], 1)
                    elif e[0] == "invT":
                        rnd, p, lv = e[1], e[2], e[3]
                        pe.wait_ge(inT_next[p], h * 10 + (5 * rnd + lv))
                        pe.wait_ge(invx[p], h * 12 + (6 * rnd + lv))
                        for c in range(4):
                            ins = te.transpose(x_bank(p, lv)[:, c * P:(c + 1) * P], inT[:, p, c], ident[:])
                        ins.then_inc(inv_yt[p], 1)

            prepare_and_finish(0, True, False)
            with pe.Fori(1, B_HEADS) as h:
                prepare_and_finish(h, False, False)
            prepare_and_finish(B_HEADS, False, True)

            for b in range(2):
                pe.wait_ge(W_free[b], W_TOTAL // 2)
            for u in range(2 * NT):
                for j in range(KT - 1 if u < FIN_EARLY else 0, KT):
                    ins = fin_sum(u, j)
                ins.then_inc(fin_full, 1)


def kernel(**inputs):
    import numpy as np
    import concourse.bacc as bacc
    from concourse.bass_utils import run_bass_kernel_spmd

    f = {k: np.asarray(v) for k, v in inputs.items()}

    def tiles(w, starts):
        w3 = w.reshape(KT, P, -1)
        return np.stack([np.concatenate([w3[:, :, a:b] for a, b in cols], axis=2).transpose(1, 0, 2) for cols in starts])

    AW, KW = A_HEADS * DH, A_GROUPS * DH
    w0 = tiles(f["attn_w_in"], [cols for g in range(A_GROUPS) for cols in (
        [(AW + g * DH, AW + (g + 1) * DH), (AW + KW + g * DH, AW + KW + (g + 1) * DH)],
        [(2 * g * P, (2 * g + 1) * P)], [((2 * g + 1) * P, (2 * g + 2) * P)],
        [(AW + 2 * KW + 2 * g * P, AW + 2 * KW + (2 * g + 1) * P)],
        [(AW + 2 * KW + (2 * g + 1) * P, AW + 2 * KW + (2 * g + 2) * P)])]).reshape(A_GROUPS, W0_TILES, P, KT, P)
    BW = B_HEADS * P
    w1 = tiles(f["delta_w_in"], [[(part + h * P, part + (h + 1) * P)] for h in range(B_HEADS)
                                 for part in (BW, 0, 2 * BW, 3 * BW)]).reshape(B_HEADS, W1_TILES, P, KT, P)
    conv = f["delta_conv"].reshape(5, 3, B_HEADS, P)[:, [1, 0, 2]].transpose(3, 2, 1, 0).reshape(P, B_HEADS * 15)
    arrays = {
        "x": f["x"].reshape(NT, P, D).transpose(1, 0, 2),
        "w0": w0,
        "wout0": f["attn_w_out"].reshape(KT, P, D).transpose(1, 0, 2),
        "w1": w1,
        "wba": f["delta_w_in"][:, 4 * BW:].reshape(KT, P, 32).transpose(1, 0, 2),
        "wout1": f["delta_w_out"].reshape(KT, P, D).transpose(1, 0, 2),
        "norm0": f["attn_norm"].reshape(KT, P).T,
        "norm1": f["delta_norm"].reshape(KT, P).T,
        "normf": f["final_norm"],
        "sink": f["attn_sink"],
        "convw": conv,
        "alog": f["delta_a_log"].reshape(16),
        "dtb": f["delta_dt_bias"].reshape(16),
        "onorm": f["delta_out_norm"].reshape(P, 1),
    }
    nc = bacc.Bacc("TRN2", target_bir_lowering=False, num_devices=1)
    sent, args = {}, []
    for name, a in arrays.items():
        sent["in_" + name] = np.ascontiguousarray(a)
        args.append(nc.dram_tensor("in_" + name, a.shape, F32, kind="ExternalInput").ap())
    args.append(nc.dram_tensor("out", (SEQ, D), F32, kind="ExternalOutput").ap())
    hybrid_encoder_kernel(nc, *args)
    r = run_bass_kernel_spmd(nc, [sent], core_ids=[0])
    return r.results[0]["out"].reshape(1, SEQ, D)
```
